# Optimizing a Trainium2 kernel written in Bass

```python
import math, functools
import jax, jax.numpy as jnp
from jax import lax
import numpy as np

D_MODEL = 1024
BATCH = 1
SEQ = 256
DEPTH = 2
DEC_BATCH = 8
DEC_SEQ = 1
PAST_LEN = 2048
PAGE_SIZE = 128

N_HEADS = 8
Q_LORA_RANK = D_MODEL // 4
KV_LORA_RANK = D_MODEL // 8
QK_NOPE_DIM = 64
QK_ROPE_DIM = 32
QK_DIM = QK_NOPE_DIM + QK_ROPE_DIM
V_HEAD_DIM = 128
ROPE_THETA = 10000.0
Q_BLOCK = 128
SM_SCALE = QK_DIM ** -0.5
CHUNK = 128
SG_GROUP_DIM = 128
SG_HALF = 3 * D_MODEL // 2
SG_GROUPS = SG_HALF // SG_GROUP_DIM
PEER_HEADS = 8
N_KEYS = 128
N_EXPERTS = N_KEYS * N_KEYS
PEER_TOPK = 16
PEER_QDIM = 256
PEER_HALF = PEER_QDIM // 2
PEER_BLOCK = 128
RMS_EPS = 1e-6

kernel_name = "hybrid_mla_chunk_sgu_peer_adaln_step"

def rms_norm(x, g):
    xf = x.astype(jnp.float32)
    y = xf * lax.rsqrt(jnp.mean(xf * xf, axis=-1, keepdims=True) + RMS_EPS)
    return y.astype(x.dtype) * g

def modulation(c, w_mod, b_mod):
    m = (jax.nn.silu(c) @ w_mod + b_mod).reshape(c.shape[0], 6, 1, D_MODEL)
    return [m[:, j] for j in range(6)]

def modulate(h, shift, scale):
    return h * (1.0 + scale) + shift

def rope_tail(x, pos):
    half = QK_ROPE_DIM // 2
    inv_freq = ROPE_THETA ** (-jnp.arange(half, dtype=jnp.float32) * 2.0 / QK_ROPE_DIM)
    ang = pos.astype(jnp.float32)[:, None] * inv_freq[None, :]
    cos = jnp.cos(ang)[:, None, :].astype(x.dtype)
    sin = jnp.sin(ang)[:, None, :].astype(x.dtype)
    x_nope = x[..., :QK_NOPE_DIM]
    x1 = x[..., QK_NOPE_DIM:QK_NOPE_DIM + half]
    x2 = x[..., QK_NOPE_DIM + half:]
    return jnp.concatenate([x_nope, x1 * cos - x2 * sin, x2 * cos + x1 * sin], axis=-1)

def mla_in(h, pos, w_in, g_q_a, g_kv_a, w_uq, g_q):
    z = h @ w_in
    cq = rms_norm(z[..., :Q_LORA_RANK], g_q_a)
    ckv = rms_norm(z[..., Q_LORA_RANK:Q_LORA_RANK + KV_LORA_RANK], g_kv_a)
    kr = z[..., Q_LORA_RANK + KV_LORA_RANK:]
    q = (cq @ w_uq).reshape(h.shape[:2] + (N_HEADS, QK_DIM))
    q = rope_tail(rms_norm(q, g_q), pos)
    return q, ckv, kr

def mla_keys(ckv, kr, k_pos, w_uk, g_k):
    kn = jnp.einsum('btc,chd->bthd', ckv, w_uk)
    kr_h = jnp.broadcast_to(kr[:, :, None, :], kn.shape[:3] + (QK_ROPE_DIM,))
    k = rms_norm(jnp.concatenate([kn, kr_h], axis=-1), g_k)
    return rope_tail(k, k_pos)

def mla_attend(q, k, ckv, q_pos, k_pos, w_uv):
    s = jnp.einsum('bqhd,bthd->bhqt', q, k).astype(jnp.float32) * SM_SCALE
    s = jnp.where(k_pos[None, :] <= q_pos[:, None], s, -jnp.inf)
    p = jax.nn.softmax(s, axis=-1).astype(ckv.dtype)
    o_lat = jnp.einsum('bhqt,btc->bqhc', p, ckv)
    return jnp.einsum('bqhc,chv->bqhv', o_lat, w_uv)

def mla_prompt(h, w_in, g_q_a, g_kv_a, w_uq, g_q, w_uk, w_uv, g_k, w_o):
    B, S, _ = h.shape
    pos = jnp.arange(S)
    q, ckv, kr = mla_in(h, pos, w_in, g_q_a, g_kv_a, w_uq, g_q)
    k = mla_keys(ckv, kr, pos, w_uk, g_k)

    def block(i):
        start = i * Q_BLOCK
        q_i = lax.dynamic_slice_in_dim(q, start, Q_BLOCK, axis=1)
        q_pos = start + jnp.arange(Q_BLOCK)
        return mla_attend(q_i, k, ckv, q_pos, pos, w_uv)

    o = lax.map(block, jnp.arange(S // Q_BLOCK))
    o = jnp.moveaxis(o, 0, 1).reshape(B, S, N_HEADS * V_HEAD_DIM)
    return o @ w_o, ckv, kr

def mla_sample(h, cache_kv, cache_kr, page_table, w_in, g_q_a, g_kv_a, w_uq, g_q, w_uk, w_uv, g_k, w_o):
    Bd, Sd, _ = h.shape
    past = page_table.shape[1] * cache_kv.shape[1]
    q_pos = past + jnp.arange(Sd)
    k_pos = jnp.arange(past + Sd)
    q, ckv, kr = mla_in(h, q_pos, w_in, g_q_a, g_kv_a, w_uq, g_q)

    def one(args):
        q_b, ckv_b, kr_b, pages = args
        ckv_all = jnp.concatenate([cache_kv[pages].reshape(past, KV_LORA_RANK), ckv_b], axis=0)[None]
        kr_all = jnp.concatenate([cache_kr[pages].reshape(past, QK_ROPE_DIM), kr_b], axis=0)[None]
        k = mla_keys(ckv_all, kr_all, k_pos, w_uk, g_k)
        return mla_attend(q_b[None], k, ckv_all, q_pos, k_pos, w_uv)[0]

    o = lax.map(one, (q, ckv, kr, page_table))
    return o.reshape(Bd, Sd, N_HEADS * V_HEAD_DIM) @ w_o, ckv, kr

def sgu_mixer(h, w_in, b_in, g_v, w_s, b_s, w_out):
    B, S, _ = h.shape
    z = jax.nn.gelu(h @ w_in + b_in)
    u = z[..., :SG_HALF]
    v = rms_norm(z[..., SG_HALF:], g_v)
    pad = (-S) % CHUNK
    n_c = (S + pad) // CHUNK
    vc = jnp.pad(v, ((0, 0), (0, pad), (0, 0))).reshape(B, n_c, CHUNK, SG_GROUPS, SG_GROUP_DIM)
    w_causal = w_s * jnp.tril(jnp.ones((CHUNK, CHUNK), w_s.dtype))
    s = jnp.einsum('gts,bcsgd->bctgd', w_causal, vc) + b_s.T[:, :, None]
    s = s.reshape(B, n_c * CHUNK, SG_HALF)[:, :S]
    return (u * s) @ w_out, v

def peer(h, w_q, sub_keys, u_tab, v_tab):
    lead = h.shape[:-1]
    xf = h.reshape(-1, D_MODEL)
    n_tok = xf.shape[0]
    pad = (-n_tok) % PEER_BLOCK
    xb = jnp.pad(xf, ((0, pad), (0, 0))).reshape(-1, PEER_BLOCK, D_MODEL)

    def block(xt):
        q = (xt @ w_q).reshape(PEER_BLOCK, PEER_HEADS, 2, PEER_HALF)
        s1 = jnp.einsum('thk,nk->thn', q[:, :, 0], sub_keys[0]).astype(jnp.float32)
        s2 = jnp.einsum('thk,nk->thn', q[:, :, 1], sub_keys[1]).astype(jnp.float32)
        t1, i1 = lax.top_k(s1, PEER_TOPK)
        t2, i2 = lax.top_k(s2, PEER_TOPK)
        cand = (t1[..., :, None] + t2[..., None, :]).reshape(PEER_BLOCK, PEER_HEADS, PEER_TOPK * PEER_TOPK)
        top, ci = lax.top_k(cand, PEER_TOPK)
        e1 = jnp.take_along_axis(i1, ci // PEER_TOPK, axis=-1)
        e2 = jnp.take_along_axis(i2, ci % PEER_TOPK, axis=-1)
        idx = e1 * N_KEYS + e2
        g = jax.nn.softmax(top, axis=-1).astype(xt.dtype)
        act = jax.nn.gelu(jnp.einsum('thkd,td->thk', u_tab[idx], xt))
        return jnp.einsum('thk,thkd->td', g * act, v_tab[idx])

    out = lax.map(block, xb).reshape(-1, D_MODEL)[:n_tok]
    return out.reshape(lead + (D_MODEL,))

def setup_inputs(seed: int = 0) -> dict:
    key = jax.random.key(seed)
    ks = iter(jax.random.split(key, 40))

    def nrm(shape, scale):
        return jax.random.normal(next(ks), shape, jnp.float32) * scale

    n_mla = (DEPTH + 1) // 2
    n_sg = DEPTH // 2
    n_pages = PAST_LEN // PAGE_SIZE
    n_used = DEC_BATCH * n_pages
    n_pool = n_used + max(1, n_used // 4)
    page_table = jax.random.permutation(next(ks), n_pool)[:n_used].reshape(DEC_BATCH, n_pages).astype(jnp.int32)
    return {
        "x_prompt": nrm((BATCH, SEQ, D_MODEL), 1.0),
        "x_sample": nrm((DEC_BATCH, DEC_SEQ, D_MODEL), 1.0),
        "c_prompt": nrm((BATCH, D_MODEL), 1.0),
        "c_sample": nrm((DEC_BATCH, D_MODEL), 1.0),
        "cache_kv_latent": nrm((n_mla, n_pool, PAGE_SIZE, KV_LORA_RANK), 1.0),
        "cache_k_rope": nrm((n_mla, n_pool, PAGE_SIZE, QK_ROPE_DIM), 1.0),
        "page_table": page_table,
        "norm1_g": 1.0 + nrm((DEPTH, D_MODEL), 0.1),
        "norm2_g": 1.0 + nrm((DEPTH, D_MODEL), 0.1),
        "w_mod": nrm((DEPTH, D_MODEL, 6 * D_MODEL), D_MODEL ** -0.5),
        "b_mod": nrm((DEPTH, 6 * D_MODEL), 0.02),
        "mla_w_in": nrm((n_mla, D_MODEL, Q_LORA_RANK + KV_LORA_RANK + QK_ROPE_DIM), D_MODEL ** -0.5),
        "mla_g_q_a": 1.0 + nrm((n_mla, Q_LORA_RANK), 0.1),
        "mla_g_kv_a": 1.0 + nrm((n_mla, KV_LORA_RANK), 0.1),
        "mla_w_uq": nrm((n_mla, Q_LORA_RANK, N_HEADS * QK_DIM), Q_LORA_RANK ** -0.5),
        "mla_g_q": 1.0 + nrm((n_mla, QK_DIM), 0.1),
        "mla_w_uk": nrm((n_mla, KV_LORA_RANK, N_HEADS, QK_NOPE_DIM), KV_LORA_RANK ** -0.5),
        "mla_w_uv": nrm((n_mla, KV_LORA_RANK, N_HEADS, V_HEAD_DIM), KV_LORA_RANK ** -0.5),
        "mla_g_k": 1.0 + nrm((n_mla, QK_DIM), 0.1),
        "mla_w_o": nrm((n_mla, N_HEADS * V_HEAD_DIM, D_MODEL), (N_HEADS * V_HEAD_DIM) ** -0.5),
        "sg_w_in": nrm((n_sg, D_MODEL, 2 * SG_HALF), D_MODEL ** -0.5),
        "sg_b_in": nrm((n_sg, 2 * SG_HALF), 0.02),
        "sg_g_v": 1.0 + nrm((n_sg, SG_HALF), 0.1),
        "sg_w_s": nrm((n_sg, SG_GROUPS, CHUNK, CHUNK), CHUNK ** -0.5),
        "sg_b_s": 1.0 + nrm((n_sg, SG_GROUPS, CHUNK), 0.1),
        "sg_w_out": nrm((n_sg, SG_HALF, D_MODEL), SG_HALF ** -0.5),
        "peer_w_q": nrm((DEPTH, D_MODEL, PEER_HEADS * PEER_QDIM), D_MODEL ** -0.5),
        "peer_sub_keys": nrm((DEPTH, 2, N_KEYS, PEER_HALF), PEER_HALF ** -0.5),
        "peer_u": nrm((DEPTH, N_EXPERTS, D_MODEL), D_MODEL ** -0.5),
        "peer_v": nrm((DEPTH, N_EXPERTS, D_MODEL), PEER_HEADS ** -0.5),
    }

def reference(x_prompt, x_sample, c_prompt, c_sample, cache_kv_latent, cache_k_rope, page_table,
              norm1_g, norm2_g, w_mod, b_mod,
              mla_w_in, mla_g_q_a, mla_g_kv_a, mla_w_uq, mla_g_q, mla_w_uk, mla_w_uv, mla_g_k, mla_w_o,
              sg_w_in, sg_b_in, sg_g_v, sg_w_s, sg_b_s, sg_w_out,
              peer_w_q, peer_sub_keys, peer_u, peer_v):
    yp, ys = x_prompt, x_sample
    kv_p, kr_p, kv_s, kr_s, v_p, v_s = [], [], [], [], [], []
    for i in range(DEPTH):
        mp = modulation(c_prompt, w_mod[i], b_mod[i])
        ms = modulation(c_sample, w_mod[i], b_mod[i])
        hp = modulate(rms_norm(yp, norm1_g[i]), mp[0], mp[1])
        hs = modulate(rms_norm(ys, norm1_g[i]), ms[0], ms[1])
        if i % 2 == 0:
            a = i // 2
            w = (mla_w_in[a], mla_g_q_a[a], mla_g_kv_a[a], mla_w_uq[a], mla_g_q[a],
                 mla_w_uk[a], mla_w_uv[a], mla_g_k[a], mla_w_o[a])
            o_p, ckv_p, krp = mla_prompt(hp, *w)
            o_s, ckv_s, krs = mla_sample(hs, cache_kv_latent[a], cache_k_rope[a], page_table, *w)
            kv_p.append(ckv_p)
            kr_p.append(krp)
            kv_s.append(ckv_s)
            kr_s.append(krs)
        else:
            b = i // 2
            w = (sg_w_in[b], sg_b_in[b], sg_g_v[b], sg_w_s[b], sg_b_s[b], sg_w_out[b])
            o_p, vp = sgu_mixer(hp, *w)
            o_s, vs = sgu_mixer(hs, *w)
            start = ((yp.shape[1] - 1) // CHUNK) * CHUNK
            v_p.append(vp[:, start:])
            v_s.append(vs)
        yp = yp + mp[2] * o_p
        ys = ys + ms[2] * o_s
        pw = (peer_w_q[i], peer_sub_keys[i], peer_u[i], peer_v[i])
        yp = yp + mp[5] * peer(modulate(rms_norm(yp, norm2_g[i]), mp[3], mp[4]), *pw)
        ys = ys + ms[5] * peer(modulate(rms_norm(ys, norm2_g[i]), ms[3], ms[4]), *pw)
    new_kv_latent_prompt = jnp.stack(kv_p)
    new_k_rope_prompt = jnp.stack(kr_p)
    new_kv_latent_sample = jnp.stack(kv_s)
    new_k_rope_sample = jnp.stack(kr_s)
    new_sg_v_prompt = jnp.stack(v_p)
    new_sg_v_sample = jnp.stack(v_s)
    return (yp, ys, new_kv_latent_prompt, new_k_rope_prompt, new_kv_latent_sample, new_k_rope_sample, new_sg_v_prompt, new_sg_v_sample)


_drawn_inputs = setup_inputs


def setup_inputs(seed=0):
    import zlib

    import numpy as np

    out = dict(_drawn_inputs(seed))
    spreads = {}
    factors = {'mla_g_q_a': 3.333, 'mla_g_q': 3.136, 'mla_g_k': 3.128, 'sg_b_in': 3.539}
    for name, (base, spread) in spreads.items():
        noise = np.random.default_rng([zlib.crc32(name.encode()), seed]).standard_normal(out[name].shape)
        drawn = base * np.exp(spread * noise) if base else spread * noise
        out[name] = __import__('jax').numpy.asarray(drawn.astype(out[name].dtype))
    for name, factor in factors.items():
        out[name] = (out[name] * factor).astype(out[name].dtype)
    return out
```

```python
from contextlib import ExitStack

import numpy as np

import concourse.bass as bass
from concourse import mybir

F32 = mybir.dt.float32
U32 = mybir.dt.uint32
I32 = mybir.dt.int32
ALU = mybir.AluOpType
ACT = mybir.ActivationFunctionType
X = mybir.AxisListType.X

P = 128
D = 1024
KD = D // P
NT = 8
H = 8
NOPE, ROPE, HALF = 64, 32, 16
QK = NOPE + ROPE
QR, KVR = 256, 128
VD = 128
PAST, PAGE = 2048, 128
SM_SCALE = QK ** -0.5
SGH = 1536
SGG = SGH // P
PH, TOPK, NKEYS = 8, 16, 128
EPS = 1e-6
NEG = -1e30
GELU_C, GELU_K = 0.044715, 0.7978845608028654
RSQRT_MAGIC = float(0x5F3759DF)

A, B, S = 0, 1, 2
ROWS = (P, P, NT)
RING = 8
WRING = 3

CONST_PARTS = [("ident", 128), ("cmask", 128), ("cmask_t", 128), ("ones", 128), ("iota16", 16), ("pmod", 1),
               ("selt", 8), ("cos_p", 32), ("sin_p", 32), ("cos_c", 256), ("sin_c", 256), ("cos_q", 16),
               ("sin_q", 16), ("own_neg", 8), ("sel16", 128)]
CONST_AT, CONST_COLS = {}, 0
for _name, _n in CONST_PARTS:
    CONST_AT[_name] = (CONST_COLS, _n)
    CONST_COLS += _n


def constants():
    c = np.zeros((P, CONST_COLS), np.float32)

    def put(name, a):
        at, n = CONST_AT[name]
        a = np.asarray(a, np.float32)
        c[:a.shape[0], at:at + n] = a.reshape(a.shape[0], n)

    p = np.arange(P)
    put("ident", np.eye(P))
    put("cmask", np.where(p[None, :] <= p[:, None], 0.0, NEG))
    put("cmask_t", (p[:, None] <= p[None, :]).astype(np.float32))
    put("ones", np.ones((P, P)))
    put("iota16", np.tile(np.arange(16), (P, 1)))
    put("pmod", (p % 16)[:, None])
    put("selt", (p[:, None] // 16 == np.arange(8)[None, :]))
    put("sel16", (p[None, :] // 16 == np.arange(8)[:, None]))
    put("own_neg", np.where(np.eye(8) > 0, 0.0, NEG))
    inv = (np.float32(10000.0) ** (-np.arange(HALF, dtype=np.float32) * np.float32(2.0) / np.float32(ROPE)))

    def angles(pos):
        return (pos.astype(np.float32)[..., None] * inv).astype(np.float32)

    for name, pos in (("p", p[:, None] + P * np.arange(2)[None, :]),
                      ("c", (np.arange(2)[None, :, None] * 1024 + 8 * p[:, None, None] + np.arange(8)[None, None, :])),
                      ("q", np.full((NT, 1), PAST))):
        a = angles(pos)
        put("cos_" + name, np.cos(a))
        put("sin_" + name, np.sin(a))
    return c


def expert_steps():
    a0, b0, a1, b1 = ([(n, h) for h in range(PH)] for n in (0, 1, 3, 4))
    return a0 + b0 + a1 + b1[:3] + [(2, None)] + b1[3:] + [(5, None)]


STEPS = expert_steps()
SLOTS = [TOPK if h is not None else PH for _, h in STEPS]


def schedule():
    s = [("init",)]
    s += [("mod", 0, j) for j in range(8)]
    s += [("norm", A, 0, 0), ("mla_in", A)]
    s += [("mod", 0, j) for j in range(8, 12)]
    s += [("attn", A), ("proj", A)]
    s += [("mod", 0, j) for j in range(12, 20)]
    s += [("norm", A, 0, 1), ("query", 0, 0)]
    fill = [[] for _ in range(len(STEPS) + 1)]
    mods = [("mod", 0, j) for j in range(20, 24)] + [("mod", 1, j) for j in range(24)]
    for h in range(1, 8):
        fill[(h - 1) // 2].append(("query", 0, h))
    fill[4] += [("norm", B, 0, 0), ("mla_in", B)]
    fill[5] += [("attn", B), ("proj", B), ("norm", B, 0, 1), ("query", 1, 0)]
    for h in range(1, 8):
        fill[6 + h // 4].append(("query", 1, h))
    for i, m in enumerate(mods):
        fill[i // 4].append(m)
    fill[8] += [("peer_out", 0), ("sgu_init",), ("norm", A, 1, 0)] + [("sgu_v", A, j) for j in range(3)]
    fill[9] += [("sgu_v", A, j) for j in range(3, 6)] + [("sgu_vnorm", A)] + [("sgu_u", A, j) for j in range(3)]
    fill[10] += [("sgu_u", A, j) for j in range(3, 6)] + [("sgu_mix", A), ("sgu_out", A)]
    fill[11] += [("norm", A, 1, 1), ("query", 3, 0), ("query", 3, 1)]
    fill[12] += [("query", 3, 2), ("query", 3, 3), ("query", 3, 4)]
    fill[13] += [("query", 3, 5), ("query", 3, 6), ("query", 3, 7)]
    fill[14] += [("norm", S, 0, 0), ("mla_in", S), ("cache_init",)]
    fill[16] += [("peer_out", 1), ("norm", B, 1, 0)] + [("sgu_v", B, j) for j in range(3)]
    fill[17] += [("sgu_v", B, j) for j in range(3, 6)] + [("sgu_vnorm", B)] + [("sgu_u", B, j) for j in range(3)]
    fill[18] += [("sgu_u", B, j) for j in range(3, 6)] + [("sgu_mix", B), ("sgu_out", B)]
    for b, p in enumerate((15, 18, 19, 20, 21, 22, 23, 24)):
        fill[p].append(("cache", b))
    fill[19] += [("norm", B, 1, 1), ("query", 4, 0), ("query", 4, 1)]
    for h in range(2, 8):
        fill[20 + (h - 2) // 2].append(("query", 4, h))
    fill[24].insert(0, ("peer_out", 3))
    fill[25] += [("cache_out",), ("proj", S), ("norm", S, 0, 1)]
    fill[26] += [("query_s", 2), ("topk_s", 2)]
    fill[28] += [("peer_out", 2), ("norm", S, 1, 0)] + [("sgu_s", j) for j in range(6)]
    fill[29] += [("sgu_s", j) for j in range(6, 12)]
    fill[30] += [("sgu_s_mix",), ("sgu_out", S), ("norm", S, 1, 1)]
    fill[31] += [("query_s", 5), ("topk_s", 5)]
    fill[33] += [("peer_out", 4)]
    fill[34] += [("peer_out", 5)]
    for p in range(len(STEPS) + 1):
        s.append(("experts", p))
        s += fill[p]
    return s


SCHEDULE = schedule()


def labels(step):
    kind, tile = step[0], step[1] if len(step) > 1 else None
    if kind == "init":
        return ["cT", "keysT", "ukT"], ["silu", "siluT", "keysT", "ukT"], ["tanh"]
    if kind == "mod":
        return ["m"], ["m"], []
    if kind == "norm":
        rep = ["rep"] if tile == S and step[3] else []
        return ["hT0", "hT1"] + rep, ["h"], ["hT0", "hT1"] + rep
    if kind == "mla_in":
        return ["z", "cT", "qk"], ["c", "kr", "qk"], ["z", "cT", "qk", "sq"]
    if kind == "attn":
        kt = range(1 + tile)
        pe, dve, act = ["qT0", "qT1", "kT0", "kT1"], ["qT0", "qT1"], ["kT0", "kT1"]
        for f in "01":
            pe += ["s" + f, *[f"pT{f}{q}" for q in kt], "ol" + f]
            dve += ["max" + f, "p" + f, "ol" + f]
            act += ["exp" + f, *[f"pT{f}{q}" for q in kt]]
        return pe + ["oT"], dve + ["oT"], act
    if kind == "cache_init":
        return (["qgT", "qabs", "qrT", "pages"], ["qg", "qr", "pages_f", "qgT", "qabs", "qpad", "pages"], [])
    if kind == "cache":
        return (["krT", "cT0", "cT1", "kn0", "kn1", "cT2", "kn2", "kn3", "cT3", "kn4", "kn5", "kn6", "kn7",
                 "maxT", "maxb", "pv"],
                ["rope", "krsq", *[f"ssn{i}" for i in range(8)], "max", "diag", "shift", "sum", "ol"],
                ["krsq", "krT", "cT0", "cT1", "sq0", "sq1", "cT2", "sq2", "sq3", "cT3", "sq4", "sq5", "sq6", "sq7",
                 "exp"])
    if kind == "cache_out":
        return ["oT"], ["oT"], []
    if kind == "proj":
        return ["w0", "w1", "w2", "w3"], ["x"], []
    if kind == "query":
        return ["q", "s"], ["top", "topk"], ["q", "s", "exp"]
    if kind == "query_s":
        return [f"q{h}" for h in range(PH)] + ["s"], [], ["q", "s"]
    if kind == "topk_s":
        return [], ["top", "topk"], ["exp"]
    if kind == "sgu_init":
        return ["wT0", "wT1", "wT2"], ["wT0", "wT1", "wT2"], []
    if kind == "sgu_v":
        return ["v"], [], ["v"]
    if kind == "sgu_vnorm":
        return [], ["poly", "v"], ["tanh"]
    if kind == "sgu_u":
        return ["u"], [], ["u"]
    if kind == "sgu_mix":
        return ["s"], ["poly", "gated"], ["tanh"]
    if kind == "sgu_s":
        return ["z"], [], ["z"]
    if kind == "sgu_s_mix":
        return ["gT"], ["poly", "v", "gated", "gT"], ["tanh"]
    if kind == "sgu_out":
        return [f"w{i}" for i in range(6)], ["x"], []
    if kind == "peer_out":
        return [], ["x"], []
    return [], [], []


PE, DVE, ACTE = 0, 1, 2


def chunk_labels(step):
    return {"mod": ["m"], "mla_in": ["z", "z", "qk"], "proj": ["w0", "w1", "w2", "w3"], "query": ["q"],
            "query_s": [f"q{h}" for h in range(PH)], "sgu_v": ["v"], "sgu_u": ["u"], "sgu_s": ["z"],
            "sgu_out": [f"w{i}" for i in range(6)]}.get(step[0], [])


BASE, CHUNK0 = [], []
_b, _c = [0, 0, 0], 0
for _s in SCHEDULE:
    BASE.append(tuple(_b))
    CHUNK0.append(_c)
    _b = [n + len(ls) for n, ls in zip(_b, labels(_s))]
    _c += len(chunk_labels(_s))
N_CHUNKS = _c
WHERE = {s: k for k, s in enumerate(SCHEDULE)}
SLOT0 = [sum(SLOTS[:p]) for p in range(len(STEPS) + 1)]
MODS = [k for k, s in enumerate(SCHEDULE) if s[0] == "mod"]
NORMS = [k for k, s in enumerate(SCHEDULE) if s[0] == "norm"]
GAINS = [k for k, s in enumerate(SCHEDULE) if s[0] in ("norm", "proj", "sgu_out", "peer_out")]
ARENA = 7680
N_ONCE = 13


def reached(e, k, name):
    return BASE[k][e] + labels(SCHEDULE[k])[e].index(name) + 1


def program(nc, t):
    with ExitStack() as ctx:
        def sb(name, shape, dt=F32):
            return ctx.enter_context(nc.sbuf_tensor(name, shape, dt))

        def psum(name, shape):
            return ctx.enter_context(nc.psum_tensor(name, shape, F32))

        def sem(name):
            return ctx.enter_context(nc.semaphore(name))

        cst = sb("cst", [P, CONST_COLS])

        def const(name, rows=P):
            at, n = CONST_AT[name]
            return cst[0:rows, at:at + n]

        ident, ones = const("ident"), const("ones")
        x = [sb(f"x{i}", [P, D]) for i in range(3)]
        hT = sb("hT", [P, KD, P])
        h_rep = sb("h_rep", [P, D])
        uring, vring = sb("uring", [P, RING, D]), sb("vring", [P, RING, D])
        wring = sb("wring", [P, WRING, 2048])
        modg, mods = sb("modg", [P, D]), sb("mods", [P, D])
        diag = sb("diag", [P, RING, P])
        expert = [sb(f"expert{i}", [P, PH, TOPK], U32) for i in range(2)]
        gate = [sb(f"gate{i}", [P, PH, TOPK]) for i in range(2)]
        expert_s, gate_s = sb("expert_s", [P, PH], U32), sb("gate_s", [P, PH])
        top_s, topi_s = sb("top_s", [64, TOPK]), sb("topi_s", [64, TOPK], U32)
        dots, wts = sb("dots", [P, 2, TOPK]), sb("wts", [P, 2, TOPK])
        ew = sb("ew", [P, 3, TOPK])
        keysT = sb("keysT", [P, 4, NKEYS])
        siluT = sb("siluT", [P, KD, 9])
        gbc = sb("gbc", [P, QR + KVR + 2 * QK])
        gqa, gkva, gqk = gbc[:, 0:QR], gbc[:, QR:QR + KVR], gbc[:, QR + KVR:QR + KVR + 2 * QK]
        w_uk, w_uv, w_ukT = sb("w_uk", [P, H * NOPE]), sb("w_uv", [P, H * VD]), sb("w_ukT", [P, 4, P])
        mrow, mbg = sb("mrow", [9, 2, 256]), sb("mbg", [9, 2, 2, 256])
        scr, rs = sb("scr", [P, 64]), sb("rs", [P, 48])
        qs = sb("qs", [P, 2, P])
        sc, work = sb("sc", [P, 2, NKEYS]), sb("work", [P, 256])
        t1, ti = sb("t1", [P, 2, TOPK]), sb("ti", [P, 2, TOPK], U32)
        cand, hot = sb("cand", [P, TOPK * TOPK]), sb("hot", [P, TOPK, TOPK])
        ctop, ci, cu = sb("ctop", [P, TOPK]), sb("ci", [P, TOPK], U32), sb("cu", [P, 2, TOPK], U32)
        cf, ef = sb("cf", [P, 4, TOPK]), sb("ef", [P, 2, TOPK])
        eg = sb("eg", [P, TOPK + 4])
        kv, kr = sb("kv", [P, 16, KVR]), sb("kr", [P, 16, ROPE])
        ptab, page_rows = sb("ptab", [NT, 16], I32), sb("page_rows", [P, 16], U32)
        ptab_f = sb("ptab_f", [NT, 16])
        ckv, krt = [sb(f"ckv{i}", [P, KVR]) for i in range(3)], [sb(f"krt{i}", [P, ROPE]) for i in range(3)]
        qabs, qpad = sb("qabs", [P, NT, H]), sb("qpad", [P, NT, 4, H])
        olS, scores, own = sb("olS", [P, H, NT]), sb("scores", [P, 17, H]), sb("own", [NT, H])
        w00 = sb("w00", [NT, 2, SGG])

        arena = sb("arena", [P, ARENA])
        taken = [0]

        def region(at):
            taken[0] = at

        def part(n):
            taken[0] += n
            assert taken[0] <= ARENA, taken[0]
            return arena[:, taken[0] - n:taken[0]]

        region(0)
        z_, cT_, qk_ = part(416), part(3 * P), part(2 * H * QK)
        kT = [part(H * P) for _ in range(2)]
        qT = part(H * P)
        att, prob = part(1024), part(1024)
        sq_, rt_ = arena[:, taken[0] - 2048:taken[0] - 512], qT
        ol, oT = qk_[:, 0:H * P], qT
        region(0)
        wcT = part(SGG * P)
        rows = part(SGH)
        sv, su, stmp = part(SGH), part(SGH), part(SGH)
        region(2 * SGH)
        krr, krT, cTc, knsq = part(16 * ROPE), part(4 * P), part(2 * 4 * P), part(2 * 1024)
        ssn, rkk, pr = part(16 * H), part(16 * H), part(17 * H)
        rope_t, krsq = knsq[:, 0:1024], knsq[:, 1024:1536]
        oTs = krr[:, 0:H * NT]
        region(2 * SGH)
        z_s, cT_s, qk_s, sq_s, rt_s = part(416), part(24), part(2 * H * QK), part(2 * H * QK), part(1024)
        h_tok = [sb("h0", [P, D]), sb("h1", [P, D]), arena[:, ARENA - D:ARENA]]

        yacc, pp, pq = psum("yacc", [P, 2, 512]), psum("pp", [P, 2, 512]), psum("pq", [P, 2, 512])
        ps = [psum("ps0", [P, 512]), psum("ps1", [P, 512])]

        stage_done = [sem("pe_stage"), sem("dve_stage"), sem("act_stage")]
        dve_chain = sem("dve_chain")
        act_chain = sem("act_chain")
        in_once, pages_in = sem("in_once"), sem("pages_in")
        w_land = [sem(f"w_land{i}") for i in range(WRING)]
        u_land, v_land = [sem(f"u_land{i}") for i in range(RING)], [sem(f"v_land{i}") for i in range(RING)]
        u_used, v_used = sem("u_used"), sem("v_used")
        poly_ready, tanh_ready, w_ready = sem("poly_ready"), sem("tanh_ready"), sem("w_ready")
        diag_ready = sem("diag_ready")
        mbias_in, mrow_out = [sem("mbias_in0"), sem("mbias_in1")], [sem("mrow_out0"), sem("mrow_out1")]
        g_land, s_land = sem("g_land"), sem("s_land")
        out_done, v_out = sem("out_done"), sem("v_out")
        route_out, route_in = sem("route_out"), sem("route_in")
        sgu_in, gv_in, w00_in, cache_in = sem("sgu_in"), sem("gv_in"), sem("w00_in"), sem("cache_in")

        def after(eng, e, k, name):
            eng.wait_ge(stage_done[e], reached(e, k, name))

        def begin(eng, k):
            kind = SCHEDULE[k][0]
            if kind in ("sgu_v", "sgu_u", "sgu_s", "mod"):
                j = k - 1
                while SCHEDULE[j][0] == "experts":
                    j -= 1
                if SCHEDULE[j][0] == kind:
                    k = j
            for e in (PE, DVE, ACTE):
                if BASE[k][e]:
                    eng.wait_ge(stage_done[e], BASE[k][e])

        class Signals:

            def __init__(self, eng, e):
                self.eng, self.e, self.k, self.n = eng, e, 0, 0

            def start(self, k):
                self.k, self.n = k, 0

            def __call__(self, ins, name):
                assert labels(SCHEDULE[self.k])[self.e][self.n] == name, (SCHEDULE[self.k], name)
                self.n += 1
                ins.then_inc(stage_done[self.e], 1)

            def end(self):
                assert self.n == len(labels(SCHEDULE[self.k])[self.e]), (SCHEDULE[self.k], self.e, self.n)

        def shape_of(tile, prompt, sample):
            return sample if tile == S else prompt

        block = ctx.enter_context(nc.Block())

        @block.sync
        def _(sp):
            def bcast(ap, r):
                return ap.to_broadcast([r, ap.shape[-1]])

            def mod_row(tile, layer, j):
                if tile == S:
                    return t["modrows"][layer, 1:9, j * D:(j + 1) * D]
                return bcast(t["modrows"][layer, 0:1, j * D:(j + 1) * D], P)

            once = ((cst[:, :], t["consts"]), (h_rep[0:1, :], t["c_prompt"]), (h_rep[1:9, :], t["c_sample"]),
                    (x[A][:, :], t["x_prompt"][0, 0:P, :]), (x[B][:, :], t["x_prompt"][0, P:2 * P, :]),
                    (x[S][0:NT, :], t["x_sample"][:, 0, :]),
                    (gqa, bcast(t["mla_g_q_a"], P)), (gkva, bcast(t["mla_g_kv_a"], P)),
                    (gqk[:, 0:QK], bcast(t["mla_g_q"], P)), (gqk[:, QK:2 * QK], bcast(t["mla_g_k"], P)),
                    (w_uk[:, :], t["mla_w_uk"][0].rearrange("c h d -> c (h d)")),
                    (w_uv[:, :], t["mla_w_uv"][0].rearrange("c h d -> c (h d)")),
                    (diag[:, 0:4, :], t["peer_sub_keys"].rearrange("l s n k -> n (l s) k")))
            assert len(once) == N_ONCE
            for dst, src in once:
                sp.dma_start(dst, src).then_inc(in_once, 16)
            for half in range(2):
                sp.dma_start(ptab[:, 8 * half:8 * half + 8],
                             t["page_table"][:, 8 * half:8 * half + 8].rearrange("b g -> g b"),
                             allow_slow_non_contiguous=True).then_inc(pages_in, 16)

            def chunk_source(k, i):
                s = SCHEDULE[k]

                def columns(w, j):
                    return w[:, 256 * j:256 * j + 256].rearrange("(k p) n -> p k n", p=P)

                def rows_of(w, i, n):
                    return w[n * i:n * i + n, :].rearrange("(k p) n -> p k n", p=P)

                if s[0] == "mod":
                    return columns(t["w_mod"][s[1]], s[2])
                if s[0] == "mla_in":
                    return rows_of(t["mla_w_in"][0], i, 512) if i < 2 else rows_of(t["mla_w_uq"][0], 0, QR)
                if s[0] == "proj":
                    return rows_of(t["mla_w_o"][0], i, 256)
                if s[0] == "sgu_out":
                    return rows_of(t["sg_w_out"][0], i, 256)
                if s[0] in ("query", "query_s"):
                    return columns(t["peer_w_q"][s[1] // 3], s[2] if s[0] == "query" else i)
                return columns(t["sg_w_in"][0], {"sgu_v": 6 + s[-1], "sgu_u": s[-1], "sgu_s": s[-1]}[s[0]])

            chunk_of = [(k, i) for k, s in enumerate(SCHEDULE) for i in range(len(chunk_labels(s)))]
            loaded = [0]

            def load_chunks(until):
                while loaded[0] < min(until, N_CHUNKS):
                    n = loaded[0]
                    src = chunk_source(*chunk_of[n])
                    if n >= WRING:
                        k, i = chunk_of[n - WRING]
                        after(sp, PE, k, chunk_labels(SCHEDULE[k])[i])
                    kk, w = src.shape[1], src.shape[2]
                    sp.dma_start(wring[:, n % WRING, 0:kk * w].rearrange("p (k n) -> p k n", k=kk), src)\
                      .then_inc(w_land[n % WRING], 16)
                    loaded[0] += 1

            def load_mod_bias(i):
                _, l, j = SCHEDULE[MODS[i]]
                if i >= 2:
                    after(sp, DVE, MODS[i - 2], "m")
                g = t["norm1_g"] if j < 12 else t["norm2_g"]
                at = 256 * (j % 4)
                sp.dma_start(mbg[:, i % 2, 0, :], bcast(t["b_mod"][l:l + 1, 256 * j:256 * j + 256], 9))\
                  .then_inc(mbias_in[i % 2], 16)
                sp.dma_start(mbg[:, i % 2, 1, :], bcast(g[l:l + 1, at:at + 256], 9)).then_inc(mbias_in[i % 2], 16)

            def mod_stored(layer, j):
                n = MODS.index(WHERE[("mod", layer, j)]) + 1
                for q in range(2):
                    sp.wait_ge(mrow_out[q], 16 * ((n + 1 - q) // 2))

            def modg_free(k):
                i = GAINS.index(k)
                if i:
                    j = GAINS[i - 1]
                    after(sp, DVE, j, "h" if SCHEDULE[j][0] == "norm" else "x")

            outs = [0]

            def store(dst, src):
                sp.dma_start(dst, src).then_inc(out_done, 16)
                outs[0] += 1

            load_mod_bias(0)
            load_mod_bias(1)
            for k, s in enumerate(SCHEDULE):
                load_chunks(CHUNK0[k] + WRING)
                kind, tile = s[0], s[1] if len(s) > 1 else None
                if kind == "mod":
                    i = MODS.index(k)
                    after(sp, DVE, k, "m")
                    sp.dma_start(t["modrows"][s[1], :, 256 * s[2]:256 * s[2] + 256], mrow[:, i % 2, :])\
                      .then_inc(mrow_out[i % 2], 16)
                    if i + 2 < len(MODS):
                        load_mod_bias(i + 2)
                elif kind == "norm":
                    _, tile, layer, second = s
                    mod_stored(layer, 12 * second + 7)
                    modg_free(k)
                    if NORMS.index(k):
                        after(sp, DVE, NORMS[NORMS.index(k) - 1], "h")
                    sp.dma_start(modg[0:ROWS[tile], :], mod_row(tile, layer, 3 * second + 1)).then_inc(g_land, 16)
                    sp.dma_start(mods[0:ROWS[tile], :], mod_row(tile, layer, 3 * second)).then_inc(s_land, 16)
                elif kind in ("proj", "sgu_out", "peer_out"):
                    layer, tile, second = (s[1] // 3, s[1] % 3, 1) if kind == "peer_out" else (int(kind == "sgu_out"), tile, 0)
                    mod_stored(layer, 12 * second + 11)
                    modg_free(k)
                    sp.dma_start(modg[0:ROWS[tile], :], mod_row(tile, layer, 3 * second + 2)).then_inc(g_land, 16)
                    if kind == "peer_out" and layer == 1:
                        after(sp, DVE, k, "x")
                        store(t["y_sample"][:, 0, :] if tile == S else t["y_prompt"][0, P * tile:P * tile + P, :],
                              x[tile][0:ROWS[tile], :])
                elif kind == "mla_in":
                    after(sp, DVE, k, "c")
                    at = slice(P * tile, P * tile + P)
                    store(t["new_kv_s"][0, :, 0, :] if tile == S else t["new_kv_p"][0, 0, at, :],
                          ckv[tile][0:ROWS[tile], :])
                    store(t["new_kr_s"][0, :, 0, :] if tile == S else t["new_kr_p"][0, 0, at, :],
                          krt[tile][0:ROWS[tile], :])
                elif kind == "sgu_init":
                    begin(sp, k)
                    sp.dma_start(sv.rearrange("p (g s) -> p g s", g=SGG), t["sg_w_s"][0].rearrange("g t s -> t g s"))\
                      .then_inc(sgu_in, 16)
                    sp.dma_start(rows[0:1, :], t["sg_b_in"][:, SGH:2 * SGH]).then_inc(sgu_in, 16)
                    sp.dma_start(rows[32:33, :], t["sg_b_in"][:, 0:SGH]).then_inc(sgu_in, 16)
                    sp.dma_start(rows[64:65, :], t["sg_b_s"].rearrange("l g t -> l (g t)")).then_inc(sgu_in, 16)
                    for i, w in enumerate((t["sg_w_s"][0, :, 0, 0:1], t["sg_b_s"][0, :, 0:1])):
                        sp.dma_start(w00[:, i, :], bcast(w.rearrange("g o -> o g"), NT),
                                     allow_slow_non_contiguous=True).then_inc(w00_in, 16)
                elif kind == "sgu_vnorm":
                    begin(sp, k)
                    sp.dma_start(su, bcast(t["sg_g_v"], P)).then_inc(gv_in, 16)
                    if tile == B:
                        after(sp, DVE, k, "v")
                        sp.dma_start(t["new_v_p"][0, 0], sv).then_inc(v_out, 16)
                elif kind == "sgu_s_mix":
                    begin(sp, k)
                    sp.dma_start(wcT[0:NT, :], bcast(t["sg_g_v"], NT)).then_inc(gv_in, 16)
                    after(sp, DVE, k, "v")
                    sp.dma_start(t["new_v_s"][0, :, 0, :], sv[0:NT, :]).then_inc(v_out, 16)
                elif kind == "topk_s":
                    i = s[1] // 3
                    after(sp, DVE, k, "topk")
                    sp.dma_start(t["route_e"][i], topi_s[:, :]).then_inc(route_out, 16)
                    sp.dma_start(t["route_g"][i], top_s[:, :]).then_inc(route_out, 16)
                    sp.wait_ge(route_out, 32 * (i + 1))
                    for b in range(NT):
                        for dst, src in ((expert_s, t["route_e"]), (gate_s, t["route_g"])):
                            sp.dma_start(dst[16 * b:16 * b + 16, :], src[i][8 * b:8 * b + 8, :].rearrange("h k -> k h"),
                                         allow_slow_non_contiguous=True).then_inc(route_in, 16)
            sp.wait_ge(out_done, 16 * outs[0])
            sp.wait_ge(v_out, 32)

        @block.gpsimd
        def _(pool):
            def gather(p, i, ring, table, used, land):
                n, h = STEPS[p]
                slot = SLOT0[p] + i
                if slot >= RING:
                    pool.wait_ge(used, slot - RING + 1)
                idx = expert_s[:, i:i + 1] if h is None else expert[n % 3][:, h, i:i + 1]
                pool.indirect_dma_start(ring[:, slot % RING, :], None, table[n // 3],
                                        bass.IndirectOffsetOnAxis(ap=idx, axis=0)).then_inc(land[slot % RING], 16)

            def gather_cache(b):
                if b == 0:
                    after(pool, DVE, WHERE[("cache_init",)], "pages")
                else:
                    for e, name in ((PE, "pv"), (DVE, "ol"), (ACTE, "exp")):
                        after(pool, e, WHERE[("cache", b - 1)], name)
                for half in range(2):
                    idx = page_rows[:, 8 * half + b:8 * half + b + 1]
                    at = slice(8 * half, 8 * half + 8)
                    for dst, src in ((kv, t["cache_kv"]), (kr, t["cache_kr"])):
                        pool.indirect_dma_start(dst[:, at, :].rearrange("p r c -> p (r c)"), None, src,
                                                bass.IndirectOffsetOnAxis(ap=idx, axis=0)).then_inc(cache_in, 16)

            cache_at = {}
            for b in range(NT):
                k = WHERE[("cache", b)]
                cache_at.setdefault(max(j for j in range(k) if SCHEDULE[j][0] == "experts"), []).append(b)
            for k, s in enumerate(SCHEDULE):
                if s[0] != "experts":
                    continue
                p = s[1]
                for b in cache_at.get(k, ()):
                    gather_cache(b)
                nu, nv = SLOTS[p] if p < len(STEPS) else 0, SLOTS[p - 1] if p else 0
                if nu:
                    n, h = STEPS[p]
                    if h is None:
                        pool.wait_ge(route_in, 16 * 2 * NT * (n // 3 + 1))
                    else:
                        after(pool, DVE, WHERE[("query", n, h)], "topk")
                for i in range(max(nu, nv)):
                    if i < nu:
                        gather(p, i, uring, t["peer_u"], u_used, u_land)
                    if i < nv:
                        gather(p - 1, i, vring, t["peer_v"], v_used, v_land)

        @block.tensor
        def _(pe):
            signal = Signals(pe, PE)

            def chunk(k, i, kk, width=2048):
                n = CHUNK0[k] + i
                pe.wait_ge(w_land[n % WRING], 16 * (n // WRING + 1))
                return wring[:, n % WRING, 0:width].rearrange("p (k n) -> p k n", k=kk)

            def transposes(out, tiles, r):
                for i, a in enumerate(tiles):
                    last = pe.transpose(out[0:a.shape[-1], r * i:r * i + r], a, ident[0:r, 0:r])
                return last

            def init(k):
                pe.wait_ge(in_once, 16 * N_ONCE)
                after(pe, DVE, k, "silu")
                for c in range(KD):
                    last = pe.transpose(ps[0][:, 16 * c:16 * c + 9], h_rep[0:9, P * c:P * c + P], ident[0:9, 0:9])
                signal(last, "cT")
                signal(transposes(ps[1], [diag[:, c, :] for c in range(4)], P), "keysT")
                signal(transposes(pp[:, 0], [w_uk[:, P * c:P * c + P] for c in range(4)], P), "ukT")

            def mod(k, l, j):
                begin(pe, k)
                w = chunk(k, 0, 8)
                out = ps[MODS.index(k) % 2]
                for c in range(KD):
                    last = pe.matmul(out[0:9, 0:256], siluT[:, c, :], w[:, c, :], start=c == 0, stop=c == KD - 1)
                signal(last, "m")

            def norm(k, tile, layer, second):
                begin(pe, k)
                after(pe, DVE, k, "h")
                r, h = ROWS[tile], h_tok[tile]
                for q in range(2):
                    signal(transposes(ps[q], [h[0:r, P * c:P * c + P] for c in range(4 * q, 4 * q + 4)], r), f"hT{q}")
                if tile == S and second:
                    for q in range(2):
                        last = pe.matmul(pp[:, q], const("sel16", NT), h[0:NT, 512 * q:512 * q + 512], start=True, stop=True)
                    signal(last, "rep")

            def mla_in(k, tile):
                begin(pe, k)
                r = ROWS[tile]
                z, cT = shape_of(tile, z_, z_s), shape_of(tile, cT_, cT_s)
                for c in range(KD):
                    w = chunk(k, c // 4, 4, 4 * 416)
                    last = pe.matmul(ps[0][0:r, 0:416], hT[:, c, 0:r], w[:, c % 4, :], start=c == 0, stop=c == KD - 1)
                signal(last, "z")
                after(pe, DVE, k, "c")
                signal(transposes(ps[1], [z[0:r, 0:P], z[0:r, P:2 * P], ckv[tile][0:r, :]], r), "cT")
                after(pe, ACTE, k, "cT")
                after(pe, ACTE, k, "z")
                w = chunk(k, 2, 2, 2 * H * QK)
                for out, a, b in ((pp[0:r, 0, 0:480], 0, 480), (pp[0:r, 1, 0:288], 480, 768)):
                    for c in range(2):
                        pe.matmul(out, cT[:, r * c:r * c + r], w[:, c, a:b], start=c == 0, stop=c == 1)
                signal(pe.matmul(ps[0][0:r, :], cT[:, 2 * r:3 * r], w_uk[:, :], start=True, stop=True), "qk")

            def attn(k, tile):
                begin(pe, k)
                kt = 1 + tile
                q3 = qk_.rearrange("p (i h d) -> p i h d", i=2, h=H)
                for i, names in enumerate((("qT0", "qT1"), ("kT0", "kT1"))):
                    for f in range(2):
                        out = ps[f] if i == 0 else pq[:, f]
                        signal(transposes(out, [q3[:, i, h, :] for h in range(4 * f, 4 * f + 4)], P), names[f])
                for f in range(2):
                    if f == 0:
                        after(pe, DVE, k, "qT1")
                        after(pe, ACTE, k, "kT1")
                    else:
                        after(pe, DVE, k, "max0")
                    for i in range(4):
                        h = 4 * f + i
                        for q in range(kt):
                            at = P * (kt * i + q)
                            last = pe.matmul(pp[:, at // 512, at % 512:at % 512 + P], qT[0:QK, P * h:P * h + P],
                                             kT[q][0:QK, P * h:P * h + P], start=True, stop=True)
                    signal(last, f"s{f}")
                    after(pe, DVE, k, f"p{f}")
                    for q in range(kt):
                        signal(transposes(ps[q], [prob[:, P * (kt * i + q):P * (kt * i + q) + P] for i in range(4)], P),
                               f"pT{f}{q}")
                    for q in range(kt):
                        after(pe, ACTE, k, f"pT{f}{q}")
                        last = pe.matmul(pq[:, f], ckv[q][:, :], att[:, 512 * q:512 * q + 512], start=q == 0, stop=q == kt - 1)
                    signal(last, f"ol{f}")
                after(pe, DVE, k, "ol1")
                for h in range(H):
                    last = pe.matmul(ps[h // 4][:, P * (h % 4):P * (h % 4) + P], w_uv[:, VD * h:VD * h + VD],
                                     ol[:, P * h:P * h + P], start=True, stop=True)
                signal(last, "oT")

            def projection(k, tile, lhs, n):
                begin(pe, k)
                r = ROWS[tile]
                for i in range(n):
                    w = chunk(k, i, 2)
                    for c in range(2):
                        g = 2 * i + c
                        for q in range(2):
                            last = pe.matmul(pp[0:r, q], lhs[:, r * g:r * g + r], w[:, c, 512 * q:512 * q + 512],
                                             start=g == 0, stop=g == 2 * n - 1)
                    signal(last, f"w{i}")

            def proj(k, tile):
                projection(k, tile, oTs if tile == S else oT, 4)

            def sgu_out(k, tile):
                projection(k, tile, su, 6)

            def query(k, n, h):
                begin(pe, k)
                w = chunk(k, 0, 8)
                for side in range(2):
                    for c in range(KD):
                        last = pe.matmul(ps[0][:, P * side:P * side + P], w[:, c, P * side:P * side + P], hT[:, c, :],
                                         start=c == 0, stop=c == KD - 1)
                signal(last, "q")
                after(pe, ACTE, k, "q")
                for side in range(2):
                    last = pe.matmul(ps[1][:, P * side:P * side + P], qs[:, side, :], keysT[:, 2 * (n // 3) + side, :],
                                     start=True, stop=True)
                signal(last, "s")

            def query_s(k, n):
                begin(pe, k)
                for h in range(PH):
                    w = chunk(k, h, 8)
                    for side in range(2):
                        at = NT * (PH * side + h)
                        for c in range(KD):
                            last = pe.matmul(ps[0][:, at:at + NT], w[:, c, P * side:P * side + P], hT[:, c, 0:NT],
                                             start=c == 0, stop=c == KD - 1)
                    signal(last, f"q{h}")
                after(pe, ACTE, k, "q")
                for side in range(2):
                    last = pe.matmul(ps[1][0:64, P * side:P * side + P], qs[:, side, 0:64],
                                     keysT[:, 2 * (n // 3) + side, :], start=True, stop=True)
                signal(last, "s")

            def cache_init(k):
                begin(pe, k)
                after(pe, DVE, k, "qg")
                signal(transposes(ps[0], [sq_s[0:NT, P * c:P * c + P] for c in range(4)], NT), "qgT")
                after(pe, DVE, k, "qgT")
                for h in range(H):
                    half = slice(64 * (h % 2), 64 * (h % 2) + 64)
                    last = pe.matmul(pq[:, h % 2, NT * (h // 2):NT * (h // 2) + NT], w_ukT[half, h // 2, :],
                                     rt_s[half, NT * (h // 2):NT * (h // 2) + NT], start=True, stop=True)
                signal(last, "qabs")
                after(pe, DVE, k, "qr")
                signal(transposes(pp[:, 0], [sq_s[0:NT, 512 + P * h:512 + P * h + P] for h in range(H)], NT), "qrT")
                after(pe, DVE, k, "pages_f")
                signal(pe.matmul(pp[:, 1, 0:16], const("sel16", NT), ptab_f[:, :], start=True, stop=True), "pages")

            def cache(k, b):
                begin(pe, k)
                pe.wait_ge(cache_in, 64 * (b + 1))
                kn_bank = (pp, pq)

                def tiles_T(g):
                    signal(transposes(ps[1], [kv[:, 4 * g + i, :] for i in range(4)], P), f"cT{g}")

                def keys_of(j):
                    if j >= 2:
                        after(pe, ACTE, k, f"sq{j - 2}")
                    for i in range(2):
                        tile = 2 * j + i
                        lhs = cTc[:, P * (tile % 8):P * (tile % 8) + P]
                        pe.matmul(kn_bank[j % 2][:, i], lhs, w_uk[:, :], start=True, stop=True)
                        last = pe.matmul(ps[0][:, H * tile:H * tile + H], lhs, qabs[:, b, :], start=False,
                                         stop=True, skip_group_check=True)
                    signal(last, f"kn{j}")

                after(pe, DVE, k, "rope")
                signal(transposes(ps[1], [krr[:, P * g:P * g + P] for g in range(4)], P), "krT")
                after(pe, ACTE, k, "krT")
                for g in range(4):
                    pe.matmul(ps[0][:, 32 * g:32 * g + 32], krT[:, P * g:P * g + P],
                              qpad[:, b].rearrange("p i h -> p (i h)"), start=g == 0, stop=False, skip_group_check=True)
                tiles_T(0)
                for g in range(4):
                    after(pe, ACTE, k, f"cT{g}")
                    if g == 0:
                        tiles_T(1)
                        keys_of(0)
                        keys_of(1)
                    else:
                        if g < 3:
                            tiles_T(g + 1)
                        keys_of(2 * g)
                        keys_of(2 * g + 1)
                after(pe, DVE, k, "max")
                signal(pe.transpose(ps[1][0:H, 0:P], scr[:, 32:40], ident), "maxT")
                after(pe, DVE, k, "diag")
                signal(pe.matmul(ps[1][:, 128:136], ones[0:H, :], scr[0:H, 48:56], start=True, stop=True), "maxb")
                after(pe, DVE, k, "sum")
                pe.matmul(ps[1][:, 256:264], ones, scr[:, 40:48], start=True, stop=True)
                for i in range(16):
                    pe.matmul(ps[1][:, 264:272], kv[:, i, :], pr[:, H * i:H * i + H], start=i == 0, stop=False)
                signal(pe.matmul(ps[1][:, 264:272], ckv[S][0:NT, :], pr[0:NT, 16 * H:17 * H], start=False, stop=True), "pv")

            def cache_out(k):
                begin(pe, k)
                for h in range(H):
                    last = pe.matmul(ps[0][:, NT * h:NT * h + NT], w_uv[:, VD * h:VD * h + VD], olS[:, h, :],
                                     start=True, stop=True)
                signal(last, "oT")

            def sgu_init(k):
                begin(pe, k)
                pe.wait_ge(sgu_in, 64)
                for q in range(3):
                    signal(transposes((ps[0], ps[1], pq[:, 0])[q], [sv[:, P * g:P * g + P] for g in range(4 * q, 4 * q + 4)], P),
                           f"wT{q}")

            def sgu_v(k, tile, j):
                begin(pe, k)
                w, out = chunk(k, 0, 8), ps[j % 2][:, 0:256]
                for c in range(KD):
                    pe.matmul(out, hT[:, c, :], w[:, c, :], start=c == 0, stop=False)
                signal(pe.matmul(out, ones[0:1, :], rows[0:1, 256 * j:256 * j + 256], start=False, stop=True), "v")

            def sgu_u(k, tile, j):
                begin(pe, k)
                w = chunk(k, 0, 8)
                for side in range(2):
                    out, at = ps[j % 2][:, P * side:P * side + P], 256 * j + P * side
                    for c in range(KD):
                        pe.matmul(out, w[:, c, P * side:P * side + P], hT[:, c, :], start=c == 0, stop=False)
                    last = pe.matmul(out, rows[32:33, at:at + P], ones[32:33, :], start=False, stop=True)
                signal(last, "u")

            def sgu_mix(k, tile):
                begin(pe, k)
                if tile == B:
                    pe.wait_ge(v_out, 16)
                for q in range(3):
                    out = (ps[0], ps[1], pq[:, 0])[q]
                    for i in range(4):
                        g, acc = 4 * q + i, out[:, P * i:P * i + P]
                        pe.matmul(acc, ones[64:65, :], rows[64:65, P * g:P * g + P], start=True, stop=False)
                        last = pe.matmul(acc, sv[:, P * g:P * g + P], wcT[:, P * g:P * g + P], start=False, stop=True)
                signal(last, "s")

            def sgu_s(k, j):
                begin(pe, k)
                w, out = chunk(k, 0, 8), ps[j % 2][0:NT, 0:256]
                part_, at = (32, 256 * j) if j < 6 else (0, 256 * j - SGH)
                for c in range(KD):
                    pe.matmul(out, hT[:, c, 0:NT], w[:, c, :], start=c == 0, stop=False)
                signal(pe.matmul(out, ones[part_:part_ + 1, 0:NT], rows[part_:part_ + 1, at:at + 256],
                                 start=False, stop=True), "z")

            def sgu_s_mix(k):
                begin(pe, k)
                pe.wait_ge(v_out, 32)
                after(pe, DVE, k, "gated")
                signal(transposes(ps[0], [stmp[0:NT, P * g:P * g + P] for g in range(SGG)], NT), "gT")

            def experts(k, p):
                if p == 0:
                    return
                n, h = STEPS[p - 1]
                if h is None:
                    begin(pe, k)
                elif h == 0 and p > 1:
                    after(pe, DVE, WHERE[("peer_out", {1: 0, 3: 1, 4: 3}[n])], "x")
                out, r = (pp, NT) if h is None else (yacc, P)
                first, final = (True, True) if h is None else (h == 0, h == PH - 1)
                for i in range(SLOTS[p - 1]):
                    slot = SLOT0[p - 1] + i
                    pe.wait_ge(v_land[slot % RING], 16 * (slot // RING + 1))
                    pe.wait_ge(diag_ready, slot + 1)
                    for q in range(2):
                        last = pe.matmul(out[0:r, q], diag[:, slot % RING, 0:r], vring[:, slot % RING, 512 * q:512 * q + 512],
                                         start=first and i == 0, stop=final and i == SLOTS[p - 1] - 1)
                    last.then_inc(v_used, 1)

            stages = dict(init=init, mod=mod, norm=norm, mla_in=mla_in, attn=attn, proj=proj, query=query,
                          query_s=query_s, cache_init=cache_init, cache=cache, cache_out=cache_out,
                          sgu_init=sgu_init, sgu_v=sgu_v, sgu_u=sgu_u, sgu_mix=sgu_mix, sgu_s=sgu_s,
                          sgu_s_mix=sgu_s_mix, sgu_out=sgu_out, experts=experts)
            for k, s in enumerate(SCHEDULE):
                signal.start(k)
                if s[0] in stages:
                    stages[s[0]](k, *s[1:])
                signal.end()

        @block.scalar
        def _(act):
            signal = Signals(act, ACTE)
            chain = [0]

            def link(ins):
                chain[0] += 1
                ins.then_inc(act_chain, 1)
                act.wait_ge(act_chain, chain[0])

            def copy(out, in_):
                return act.activation(out, in_, ACT.Copy)

            def init(k):
                act.wait_ge(in_once, 16 * N_ONCE)
                signal(act.activation(h_tok[A][0:9, :], h_rep[0:9, :], ACT.Tanh, scale=0.5), "tanh")

            def norm(k, tile, layer, second):
                begin(act, k)
                r = ROWS[tile]
                for q in range(2):
                    after(act, PE, k, f"hT{q}")
                    signal(copy(hT[:, 4 * q:4 * q + 4, 0:r], ps[q][:, 0:4 * r].rearrange("p (c t) -> p c t", c=4)), f"hT{q}")
                if tile == S and second:
                    after(act, PE, k, "rep")
                    signal(copy(h_rep[:, :], pp[:, :, :].rearrange("p q n -> p (q n)")), "rep")

            def mla_in(k, tile):
                begin(act, k)
                r = ROWS[tile]
                z, cT, qk, sq = (shape_of(tile, a, b) for a, b in ((z_, z_s), (cT_, cT_s), (qk_, qk_s), (sq_, sq_s)))
                after(act, PE, k, "z")
                signal(copy(z[0:r, :], ps[0][0:r, 0:416]), "z")
                after(act, PE, k, "cT")
                signal(copy(cT[:, 0:3 * r], ps[1][:, 0:3 * r]), "cT")
                after(act, PE, k, "qk")
                copy(qk[0:r, 0:480], pp[0:r, 0, 0:480])
                copy(qk[0:r, 480:768], pp[0:r, 1, 0:288])
                keys = qk[0:r, 768:1536].rearrange("p (h d) -> p h d", h=H)
                signal(copy(keys[:, :, 0:NOPE], ps[0][0:r, :].rearrange("p (h d) -> p h d", h=H)), "qk")
                after(act, ACTE, k, "qk")
                after(act, DVE, k, "kr")
                signal(act.activation(sq[0:r, :], qk[0:r, :], ACT.Square), "sq")

            def attn(k, tile):
                begin(act, k)
                kt = 1 + tile
                for f in range(2):
                    after(act, PE, k, f"kT{f}")
                    signal(copy(kT[tile][0:QK, 512 * f:512 * f + 512], pq[0:QK, f]), f"kT{f}")
                for f in range(2):
                    after(act, DVE, k, f"max{f}")
                    n = P * kt
                    for i in range(4):
                        last = act.activation(prob[:, n * i:n * i + n], att[:, n * i:n * i + n], ACT.Exp,
                                              bias=scr[:, 4 + i:5 + i], scale=SM_SCALE, accum_out=scr[:, 8 + i:9 + i])
                    signal(last, f"exp{f}")
                    for q in range(kt):
                        after(act, PE, k, f"pT{f}{q}")
                        signal(copy(att[:, 512 * q:512 * q + 512], ps[q][:, :]), f"pT{f}{q}")

            def query(k, n, h):
                begin(act, k)
                after(act, PE, k, "q")
                signal(copy(qs[:, :, :], ps[0][:, 0:256].rearrange("p (i t) -> p i t", i=2)), "q")
                after(act, PE, k, "s")
                signal(copy(sc[:, :, :], ps[1][:, 0:256].rearrange("p (i t) -> p i t", i=2)), "s")
                pick_exp(k, P)

            def pick_exp(k, r):
                after(act, DVE, k, "top")
                signal(act.activation(eg[0:r, 0:TOPK], ctop[0:r, :], ACT.Exp, bias=eg[0:r, TOPK:TOPK + 1],
                                      accum_out=eg[0:r, TOPK + 1:TOPK + 2]), "exp")

            def query_s(k, n):
                begin(act, k)
                after(act, PE, k, f"q{PH - 1}")
                for side in range(2):
                    last = copy(qs[:, side, 0:64].rearrange("p (b h) -> p h b", h=PH),
                                ps[0][:, 64 * side:64 * side + 64].rearrange("p (h b) -> p h b", h=PH))
                signal(last, "q")
                after(act, PE, k, "s")
                signal(copy(sc[0:64, :, :], ps[1][0:64, 0:256].rearrange("p (i t) -> p i t", i=2)), "s")

            def topk_s(k, n):
                begin(act, k)
                pick_exp(k, 64)

            def cache(k, b):
                begin(act, k)
                act.wait_ge(cache_in, 64 * (b + 1))
                kn_bank = (pp, pq)
                after(act, DVE, k, "rope")
                signal(act.activation(krsq, kr[:, :, :].rearrange("p r j -> p (r j)"), ACT.Square), "krsq")
                after(act, PE, k, "krT")
                signal(copy(krT, ps[1][:, :]), "krT")

                def latents(g):
                    after(act, PE, k, f"cT{g}")
                    if g >= 2:
                        after(act, PE, k, f"kn{2 * g - 3}")
                    signal(copy(cTc[:, 512 * (g % 2):512 * (g % 2) + 512], ps[1][:, :]), f"cT{g}")

                def squares(j):
                    after(act, PE, k, f"kn{j}")
                    if j < 2:
                        after(act, DVE, k, "krsq")
                    else:
                        after(act, DVE, k, f"ssn{j - 2}")
                    signal(act.activation(knsq[:, 1024 * (j % 2):1024 * (j % 2) + 1024],
                                          kn_bank[j % 2][:, :, :].rearrange("p i n -> p (i n)"), ACT.Square), f"sq{j}")

                latents(0)
                for g in range(4):
                    if g < 3:
                        latents(g + 1)
                    squares(2 * g)
                    squares(2 * g + 1)
                after(act, DVE, k, "shift")
                signal(act.activation(pr, pr, ACT.Exp, scale=SM_SCALE), "exp")

            def sgu_v(k, tile, j):
                begin(act, k)
                after(act, PE, k, "v")
                signal(copy(sv[:, 256 * j:256 * j + 256], ps[j % 2][:, 0:256]), "v")

            def sgu_vnorm(k, tile):
                begin(act, k)
                after(act, DVE, k, "poly")
                signal(act.activation(stmp, stmp, ACT.Tanh, scale=GELU_K), "tanh")

            def sgu_u(k, tile, j):
                begin(act, k)
                after(act, PE, k, "u")
                signal(copy(su[:, 256 * j:256 * j + 256], ps[j % 2][:, 0:256]), "u")

            def sgu_s(k, j):
                begin(act, k)
                after(act, PE, k, "z")
                dst = su[0:NT, 256 * j:256 * j + 256] if j < 6 else sv[0:NT, 256 * j - SGH:256 * j - SGH + 256]
                signal(copy(dst, ps[j % 2][0:NT, 0:256]), "z")

            def sgu_s_mix(k):
                begin(act, k)
                after(act, DVE, k, "poly")
                act.activation(stmp[0:NT, :], stmp[0:NT, :], ACT.Tanh, scale=GELU_K)
                signal(act.activation(rows[0:NT, :], rows[0:NT, :], ACT.Tanh, scale=GELU_K), "tanh")

            def experts(k, p):
                if p:
                    act.wait_ge(w_ready, p)
                    h = STEPS[p - 1][1]
                    base = const("selt") if h is None else ident
                    for i in range(SLOTS[p - 1]):
                        slot = SLOT0[p - 1] + i
                        if slot >= RING:
                            act.wait_ge(v_used, slot - RING + 1)
                        act.activation(diag[:, slot % RING, 0:base.shape[-1]], base, ACT.Copy,
                                       scale=wts[:, (p - 1) % 2, i:i + 1]).then_inc(diag_ready, 1)
                if p < len(STEPS):
                    n = SLOTS[p]
                    act.wait_ge(poly_ready, p + 1)
                    act.activation(ew[:, 2, 0:n], ew[:, 0, 0:n], ACT.Tanh, scale=GELU_K).then_inc(tanh_ready, 1)

            stages = dict(init=init, norm=norm, mla_in=mla_in, attn=attn, query=query, query_s=query_s, topk_s=topk_s,
                          cache=cache, sgu_v=sgu_v, sgu_vnorm=sgu_vnorm, sgu_u=sgu_u, sgu_mix=sgu_vnorm,
                          sgu_s=sgu_s, sgu_s_mix=sgu_s_mix, experts=experts)
            for k, s in enumerate(SCHEDULE):
                signal.start(k)
                if s[0] in stages:
                    stages[s[0]](k, *s[1:])
                signal.end()

        @block.vector
        def _(dve):
            signals = Signals(dve, DVE)
            chain = [0]

            def link(ins):
                chain[0] += 1
                ins.then_inc(dve_chain, 1)
                dve.wait_ge(dve_chain, chain[0])

            def signal(ins, name):
                signals(ins, name)
                after(dve, DVE, signals.k, name)

            tt, ts, stt, cp = dve.tensor_tensor, dve.tensor_scalar, dve.scalar_tensor_tensor, dve.tensor_copy

            def over(a, n):
                return a.unsqueeze(2).to_broadcast([a.shape[0], a.shape[1], n])

            def times(a, n):
                return a.unsqueeze(1).to_broadcast([a.shape[0], n, a.shape[1]])

            def rsqrt(out, v, tmp):
                link(ts(out.bitcast(U32), v.bitcast(U32), 1, None, ALU.logical_shift_right))
                link(ts(out.bitcast(U32), out.bitcast(U32), -1.0, RSQRT_MAGIC, ALU.mult, ALU.add))
                for _ in range(3):
                    link(tt(tmp, out, out, ALU.mult))
                    link(tt(tmp, tmp, v, ALU.mult))
                    link(ts(tmp, tmp, -0.5, 1.5, ALU.mult, ALU.add))
                    link(tt(out, out, tmp, ALU.mult))

            def square_sum(out, a, waste):
                link(dve.tensor_tensor_reduce(waste, a, a, 1.0, 0.0, ALU.mult, ALU.add, out))

            def init(k):
                dve.wait_ge(in_once, 16 * N_ONCE)
                after(dve, ACTE, k, "tanh")
                c, th = h_rep[0:9, :], h_tok[A][0:9, :]
                link(stt(c, th, 1.0, c, ALU.add, ALU.mult))
                signal(ts(c, c, 0.5, None, ALU.mult), "silu")
                after(dve, PE, k, "cT")
                signal(cp(siluT[:, :, :], ps[0][:, 0:16 * KD].rearrange("p (c t) -> p c t", c=KD)[:, :, 0:9]), "siluT")
                after(dve, PE, k, "keysT")
                signal(cp(keysT[:, :, :].rearrange("p i n -> p (i n)"), ps[1][:, :]), "keysT")
                after(dve, PE, k, "ukT")
                signal(cp(w_ukT[:, :, :].rearrange("p i n -> p (i n)"), pp[:, 0]), "ukT")

            def mod(k, l, j):
                begin(dve, k)
                i = MODS.index(k)
                after(dve, PE, k, "m")
                dve.wait_ge(mbias_in[i % 2], 32 * (i // 2 + 1))
                if i >= 2:
                    dve.wait_ge(mrow_out[i % 2], 16 * (i // 2))
                out, acc = mrow[:, i % 2, :], ps[i % 2][0:9, 0:256]
                if j // 4 in (1, 4):
                    link(tt(out, acc, mbg[:, i % 2, 0, :], ALU.add))
                    signal(stt(out, out, 1.0, mbg[:, i % 2, 1, :], ALU.add, ALU.mult), "m")
                else:
                    signal(tt(out, acc, mbg[:, i % 2, 0, :], ALU.add), "m")

            def norm(k, tile, layer, second):
                begin(dve, k)
                r, n = ROWS[tile], NORMS.index(k)
                xr, h = x[tile][0:r, :], h_tok[tile][0:r, :]
                square_sum(scr[0:r, 0:1], xr, h)
                link(ts(scr[0:r, 0:1], scr[0:r, 0:1], 1.0 / D, EPS, ALU.mult, ALU.add))
                rsqrt(scr[0:r, 1:2], scr[0:r, 0:1], rs[0:r, 0:1])
                dve.wait_ge(g_land, 16 * (GAINS.index(k) + 1))
                link(stt(h, xr, scr[0:r, 1:2], modg[0:r, :], ALU.mult, ALU.mult))
                dve.wait_ge(s_land, 16 * (n + 1))
                signal(tt(h, h, mods[0:r, :], ALU.add), "h")

            def rotate(a, cos, sin, tmp, out=None):
                n = a.shape[1]
                x1, x2 = a[:, :, 0:HALF], a[:, :, HALF:ROPE]
                m = [tmp[:, HALF * n * i:HALF * n * (i + 1)].rearrange("p (n j) -> p n j", n=n) for i in range(4)]
                link(tt(m[0], x1, cos, ALU.mult))
                link(tt(m[1], x2, sin, ALU.mult))
                link(tt(m[2], x2, cos, ALU.mult))
                link(tt(m[3], x1, sin, ALU.mult))
                link(tt(x1, m[0], m[1], ALU.subtract))
                return tt(x2, m[2], m[3], ALU.add)

            def mla_in(k, tile):
                begin(dve, k)
                r = ROWS[tile]
                z, qk, sq, rt = (shape_of(tile, a, b)[0:r, :] for a, b in ((z_, z_s), (qk_, qk_s), (sq_, sq_s), (rt_, rt_s)))
                after(dve, ACTE, k, "z")
                square_sum(scr[0:r, 0:1], z[:, 0:QR], sq[:, 0:QR])
                square_sum(scr[0:r, 1:2], z[:, QR:QR + KVR], sq[:, 0:KVR])
                link(ts(scr[0:r, 0:1], scr[0:r, 0:1], 1.0 / QR, EPS, ALU.mult, ALU.add))
                link(ts(scr[0:r, 1:2], scr[0:r, 1:2], 1.0 / KVR, EPS, ALU.mult, ALU.add))
                rsqrt(scr[0:r, 2:4], scr[0:r, 0:2], rs[0:r, 0:2])
                link(cp(krt[tile][0:r, :], z[:, QR + KVR:416]))
                link(stt(z[:, 0:QR], z[:, 0:QR], scr[0:r, 2:3], gqa[0:r, :], ALU.mult, ALU.mult))
                signal(stt(ckv[tile][0:r, :], z[:, QR:QR + KVR], scr[0:r, 3:4], gkva[0:r, :], ALU.mult, ALU.mult), "c")
                q4 = qk.rearrange("p (i h d) -> p i h d", i=2, h=H)
                q3 = qk.rearrange("p (i d) -> p i d", i=2 * H)
                signal(cp(q4[:, 1, :, NOPE:QK], times(krt[tile][0:r, :], H)), "kr")
                after(dve, ACTE, k, "sq")
                s16, v16 = scr[0:r, 16:32], scr[0:r, 32:48]
                link(dve.tensor_reduce(v16, sq.rearrange("p (i d) -> p i d", i=2 * H), X, ALU.add))
                link(ts(v16, v16, 1.0 / QK, EPS, ALU.mult, ALU.add))
                rsqrt(s16, v16, rs[0:r, 0:16])
                link(tt(q3, q3, over(s16, QK), ALU.mult))
                for i in range(2):
                    link(tt(q4[:, i], q4[:, i], times(gqk[0:r, QK * i:QK * i + QK], H), ALU.mult))
                if tile == S:
                    cos, sin = const("cos_q", r), const("sin_q", r)
                else:
                    cos, sin = (const(c)[:, HALF * tile:HALF * tile + HALF] for c in ("cos_p", "sin_p"))
                signal(rotate(q3[:, :, NOPE:QK], times(cos, 2 * H), times(sin, 2 * H), rt), "qk")

            def attn(k, tile):
                begin(dve, k)
                kt = 1 + tile
                for f in range(2):
                    after(dve, PE, k, f"qT{f}")
                    signal(cp(qT[0:QK, 512 * f:512 * f + 512], ps[f][0:QK, :]), f"qT{f}")
                for f in range(2):
                    after(dve, PE, k, f"s{f}")
                    s4 = pp[:, :, :].rearrange("p q n -> p (q n)")[:, 0:512 * kt].rearrange("p (h q k) -> p h q k", h=4, q=kt)
                    a4 = att[:, 0:512 * kt].rearrange("p (h q k) -> p h q k", h=4, q=kt)
                    if f:
                        after(dve, PE, k, "ol0")
                    if kt == 2:
                        link(cp(a4[:, :, 0], s4[:, :, 0]))
                    link(tt(a4[:, :, kt - 1], s4[:, :, kt - 1], times(const("cmask"), 4), ALU.add))
                    link(dve.tensor_reduce(scr[:, 0:4], att[:, 0:512 * kt].rearrange("p (h n) -> p h n", h=4), X, ALU.max))
                    signal(ts(scr[:, 4:8], scr[:, 0:4], -SM_SCALE, None, ALU.mult), f"max{f}")
                    after(dve, ACTE, k, f"exp{f}")
                    link(dve.reciprocal(scr[:, 12:16], scr[:, 8:12]))
                    p3 = prob[:, 0:512 * kt].rearrange("p (h n) -> p h n", h=4)
                    signal(tt(p3, p3, over(scr[:, 12:16], P * kt), ALU.mult), f"p{f}")
                    after(dve, PE, k, f"ol{f}")
                    signal(cp(ol[:, 512 * f:512 * f + 512], pq[:, f]), f"ol{f}")
                after(dve, PE, k, "oT")
                link(cp(oT[:, 0:512], ps[0][:, :]))
                signal(cp(oT[:, 512:1024], ps[1][:, :]), "oT")

            def residual(k, tile, acc):
                r = ROWS[tile]
                dve.wait_ge(g_land, 16 * (GAINS.index(k) + 1))
                h = h_tok[tile][0:r, :]
                link(tt(h, acc[0:r, :, :].rearrange("p q n -> p (q n)"), modg[0:r, :], ALU.mult))
                signal(tt(x[tile][0:r, :], x[tile][0:r, :], h, ALU.add), "x")

            def proj(k, tile):
                begin(dve, k)
                after(dve, PE, k, "w3")
                residual(k, tile, pp)

            def sgu_out(k, tile):
                begin(dve, k)
                after(dve, PE, k, "w5")
                residual(k, tile, pp)

            def peer_out(k, n):
                begin(dve, k)
                last = max(p for p, s in enumerate(STEPS) if s[0] == n)
                dve.wait_ge(v_used, SLOT0[last + 1])
                residual(k, n % 3, pp if n % 3 == S else yacc)

            def top16(vals, index, a, scratch, r):
                link(dve.max(vals[:, 0:8], a))
                link(dve.match_replace(scratch, vals[:, 0:8], a, -3e38))
                link(dve.max_index(index[:, 0:8], vals[:, 0:8], a))
                link(dve.max(vals[:, 8:16], scratch))
                link(dve.max_index(index[:, 8:16], vals[:, 8:16], scratch))

            def route(k, r, expert_out, gate_out):
                for i in range(2):
                    top16(t1[0:r, i, :], ti[0:r, i, :], sc[0:r, i, :], work[0:r, 0:NKEYS], r)
                c3 = cand[0:r, :].rearrange("p (a b) -> p a b", a=TOPK)
                link(tt(c3, over(t1[0:r, 0, :], TOPK), times(t1[0:r, 1, :], TOPK), ALU.add))
                top16(ctop[0:r, :], ci[0:r, :], cand[0:r, :], work[0:r, :], r)
                signal(ts(eg[0:r, TOPK:TOPK + 1], ctop[0:r, 0:1], -1.0, None, ALU.mult), "top")
                link(ts(cu[0:r, 0, :], ci[0:r, :], 4, None, ALU.logical_shift_right))
                link(ts(cu[0:r, 1, :], ci[0:r, :], 15, None, ALU.bitwise_and))
                link(cp(cf[0:r, 0:2, :], cu[0:r, :, :]))
                link(cp(cf[0:r, 2:4, :], ti[0:r, :, :]))
                for i in range(2):
                    hr = hot[0:r, :, :]
                    link(tt(hr, over(cf[0:r, i, :], TOPK), times(const("iota16", r), TOPK), ALU.is_equal))
                    link(tt(hr, hr, times(cf[0:r, 2 + i, :], TOPK), ALU.mult))
                    link(dve.tensor_reduce(ef[0:r, i, :], hr, X, ALU.add))
                link(stt(expert_out, ef[0:r, 0, :], float(NKEYS), ef[0:r, 1, :], ALU.mult, ALU.add))
                after(dve, ACTE, k, "exp")
                link(dve.reciprocal(eg[0:r, TOPK + 2:TOPK + 3], eg[0:r, TOPK + 1:TOPK + 2]))
                signal(ts(gate_out, eg[0:r, 0:TOPK], eg[0:r, TOPK + 2:TOPK + 3], 0.5, ALU.mult, ALU.mult), "topk")

            def query(k, n, h):
                begin(dve, k)
                after(dve, ACTE, k, "s")
                route(k, P, expert[n % 3][:, h, :], gate[n % 3][:, h, :])

            def topk_s(k, n):
                begin(dve, k)
                route(k, 64, topi_s[:, :], top_s[:, :])

            def cache_init(k):
                begin(dve, k)
                q4 = qk_s[0:NT, :].rearrange("p (i h d) -> p i h d", i=2, h=H)
                q, key = q4[:, 0], q4[:, 1]
                gn = times(gqk[0:NT, QK:QK + NOPE], H)
                signal(tt(sq_s[0:NT, 0:512].rearrange("p (h d) -> p h d", h=H), q[:, :, 0:NOPE], gn, ALU.mult), "qg")
                rep = sq_s[0:NT, 512:1536].rearrange("p (h i j) -> p h i j", h=H, i=4)
                for i in range(3):
                    link(cp(rep[:, :, i], q[:, :, NOPE:QK]))
                signal(cp(rep[:, :, 3], q[:, :, NOPE:QK]), "qr")
                dve.wait_ge(pages_in, 32)
                signal(cp(ptab_f[:, :], ptab[:, :]), "pages_f")
                m = rt_s[0:NT, 0:H * QK].rearrange("p (h d) -> p h d", h=H)
                link(tt(m, q, key, ALU.mult))
                link(dve.tensor_reduce(own[:, :], m, X, ALU.add))
                link(dve.memset(scores[:, :, :], NEG))
                link(dve.memset(qpad[:, :, :, :], 0.0))
                after(dve, PE, k, "qgT")
                signal(cp(rt_s[:, 0:32], ps[0][:, 0:32]), "qgT")
                after(dve, PE, k, "qabs")
                for i in range(2):
                    ins = cp(qabs[:, :, :].rearrange("p b (h i) -> p i h b", i=2)[:, i],
                             pq[:, i, 0:32].rearrange("p (h b) -> p h b", h=4))
                    if i == 0:
                        link(ins)
                signal(ins, "qabs")
                after(dve, PE, k, "qrT")
                for i in range(4):
                    at = slice(32 * i, 32 * i + 32)
                    ins = cp(qpad[at, :, i, :].rearrange("p b h -> p h b"),
                             pp[at, 0, 0:64].rearrange("p (h b) -> p h b", h=H))
                    if i < 3:
                        link(ins)
                signal(ins, "qpad")
                after(dve, PE, k, "pages")
                signal(ts(page_rows[:, :], pp[:, 1, 0:16], 16.0, const("pmod"), ALU.mult, ALU.add), "pages")

            def cache(k, b):
                begin(dve, k)
                dve.wait_ge(cache_in, 64 * (b + 1))
                r3 = krr.rearrange("p (t j) -> p t j", t=16)
                link(tt(r3, kr[:, :, :], times(gqk[:, QK + NOPE:2 * QK], 16), ALU.mult))
                cos, sin = (const(c).rearrange("p (t j) -> p t j", t=16) for c in ("cos_c", "sin_c"))
                signal(rotate(r3, cos, sin, rope_t), "rope")
                after(dve, ACTE, k, "krsq")
                signal(dve.tensor_reduce(scr[:, 16:32], krsq.rearrange("p (t j) -> p t j", t=16), X, ALU.add), "krsq")
                for j in range(8):
                    after(dve, ACTE, k, f"sq{j}")
                    signal(dve.tensor_reduce(ssn[:, 16 * j:16 * j + 16],
                                             knsq[:, 1024 * (j % 2):1024 * (j % 2) + 1024].rearrange("p (i d) -> p i d", d=NOPE),
                                             X, ALU.add), f"ssn{j}")
                n3 = ssn.rearrange("p (t h) -> p t h", t=16)
                link(tt(n3, n3, over(scr[:, 16:32], H), ALU.add))
                link(ts(ssn, ssn, 1.0 / QK, EPS, ALU.mult, ALU.add))
                rsqrt(rkk, ssn, pr[:, 0:128])
                after(dve, PE, k, "kn7")
                link(tt(scores[:, 0:16, :].rearrange("p t h -> p (t h)"), ps[0][:, 0:128], rkk, ALU.mult))
                link(ts(scores[0:NT, 16, :], own[:, :], const("own_neg", NT)[:, b:b + 1], None, ALU.add))
                signal(dve.tensor_reduce(scr[:, 32:40], scores[:, :, :].rearrange("p t h -> p h t"), X, ALU.max), "max")
                after(dve, PE, k, "maxT")
                link(dve.tensor_reduce(scr[0:H, 56:57], ps[1][0:H, 0:P], X, ALU.max))
                signal(ts(scr[0:H, 48:56], ident[0:H, 0:H], scr[0:H, 56:57], None, ALU.mult), "diag")
                after(dve, PE, k, "maxb")
                link(cp(scr[:, 0:8], ps[1][:, 128:136]))
                p3 = pr.rearrange("p (t h) -> p t h", t=17)
                signal(tt(p3, scores[:, :, :], times(scr[:, 0:8], 17), ALU.subtract), "shift")
                after(dve, ACTE, k, "exp")
                signal(dve.tensor_reduce(scr[:, 40:48], pr.rearrange("p (t h) -> p h t", t=17), X, ALU.add), "sum")
                after(dve, PE, k, "pv")
                link(dve.reciprocal(scr[:, 8:16], ps[1][:, 256:264]))
                signal(tt(olS[:, :, b], ps[1][:, 264:272], scr[:, 8:16], ALU.mult), "ol")

            def cache_out(k):
                begin(dve, k)
                after(dve, PE, k, "oT")
                signal(cp(oTs, ps[0][:, 0:64]), "oT")

            def sgu_init(k):
                begin(dve, k)
                for q in range(3):
                    after(dve, PE, k, f"wT{q}")
                    out = (ps[0], ps[1], pq[:, 0])[q]
                    signal(tt(wcT[:, 512 * q:512 * q + 512].rearrange("p (g t) -> p g t", g=4),
                              out[:, :].rearrange("p (g t) -> p g t", g=4), times(const("cmask_t"), 4), ALU.mult), f"wT{q}")

            def polynomial(out, a):
                link(tt(out, a, a, ALU.mult))
                link(ts(out, out, GELU_C, 1.0, ALU.mult, ALU.add))
                return tt(out, out, a, ALU.mult)

            def norm_v(r, waste, g, name):
                v = sv[0:r, :]
                square_sum(scr[0:r, 0:1], v, waste)
                link(ts(scr[0:r, 0:1], scr[0:r, 0:1], 0.25 / SGH, EPS, ALU.mult, ALU.add))
                rsqrt(scr[0:r, 1:2], scr[0:r, 0:1], rs[0:r, 0:1])
                link(ts(scr[0:r, 2:3], scr[0:r, 1:2], 0.5, None, ALU.mult))
                signal(stt(v, v, scr[0:r, 2:3], g, ALU.mult, ALU.mult), name)

            def sgu_vnorm(k, tile):
                begin(dve, k)
                signal(polynomial(stmp, sv), "poly")
                after(dve, ACTE, k, "tanh")
                link(stt(sv, stmp, 1.0, sv, ALU.add, ALU.mult))
                dve.wait_ge(gv_in, 16 * (tile + 1))
                norm_v(P, stmp, su, "v")

            def sgu_mix(k, tile):
                begin(dve, k)
                signal(polynomial(stmp, su), "poly")
                after(dve, ACTE, k, "tanh")
                link(stt(su, stmp, 1.0, su, ALU.add, ALU.mult))
                after(dve, PE, k, "s")
                for q in range(3):
                    at = slice(512 * q, 512 * q + 512)
                    ins = stt(su[:, at], (ps[0], ps[1], pq[:, 0])[q][:, :], 0.5, su[:, at], ALU.mult, ALU.mult)
                    if q < 2:
                        link(ins)
                signal(ins, "gated")

            def sgu_s_mix(k):
                begin(dve, k)
                r = slice(0, NT)
                link(polynomial(stmp[r, :], su[r, :]))
                signal(polynomial(rows[r, :], sv[r, :]), "poly")
                after(dve, ACTE, k, "tanh")
                link(stt(su[r, :], stmp[r, :], 1.0, su[r, :], ALU.add, ALU.mult))
                link(stt(sv[r, :], rows[r, :], 1.0, sv[r, :], ALU.add, ALU.mult))
                dve.wait_ge(gv_in, 48)
                norm_v(NT, stmp[r, :], wcT[r, :], "v")
                dve.wait_ge(w00_in, 32)
                s3, v3 = (a[r, :].rearrange("p (g c) -> p g c", g=SGG) for a in (stmp, sv))
                link(tt(s3, v3, over(w00[:, 0, :], P), ALU.mult))
                link(tt(s3, s3, over(w00[:, 1, :], P), ALU.add))
                signal(stt(stmp[r, :], stmp[r, :], 0.5, su[r, :], ALU.mult, ALU.mult), "gated")
                after(dve, PE, k, "gT")
                signal(cp(su[:, 0:SGG * NT], ps[0][:, 0:SGG * NT]), "gT")

            def experts(k, p):
                if p == len(STEPS):
                    return
                n, h = STEPS[p]
                m, tile = SLOTS[p], n % 3
                rows_h = h_rep if tile == S else h_tok[tile]
                if tile == S:
                    after(dve, ACTE, WHERE[("norm", S, n // 3, 1)], "rep")
                    dve.wait_ge(route_in, 32 * NT * (n // 3 + 1))
                for i in range(m):
                    slot = SLOT0[p] + i
                    dve.wait_ge(u_land[slot % RING], 16 * (slot // RING + 1))
                    u = uring[:, slot % RING, :]
                    dve.tensor_tensor_reduce(u, u, rows_h[:, :], 1.0, 0.0, ALU.mult, ALU.add,
                                             dots[:, p % 2, i:i + 1]).then_inc(u_used, 1)
                dve.wait_ge(u_used, SLOT0[p + 1])
                d = dots[:, p % 2, 0:m]
                polynomial(ew[:, 0, 0:m], d).then_inc(poly_ready, 1)
                g = gate_s[:, :] if h is None else gate[tile][:, h, :]
                link(tt(ew[:, 1, 0:m], d, g, ALU.mult))
                dve.wait_ge(tanh_ready, p + 1)
                if p >= 2:
                    dve.wait_ge(diag_ready, SLOT0[p - 1])
                stt(wts[:, p % 2, 0:m], ew[:, 2, 0:m], 1.0, ew[:, 1, 0:m], ALU.add, ALU.mult).then_inc(w_ready, 1)

            stages = dict(init=init, mod=mod, norm=norm, mla_in=mla_in, attn=attn, proj=proj, query=query, topk_s=topk_s,
                          cache_init=cache_init, cache=cache, cache_out=cache_out, sgu_init=sgu_init,
                          sgu_vnorm=sgu_vnorm, sgu_mix=sgu_mix, sgu_s_mix=sgu_s_mix, sgu_out=sgu_out,
                          peer_out=peer_out, experts=experts)
            for k, s in enumerate(SCHEDULE):
                signals.start(k)
                if s[0] in stages:
                    stages[s[0]](k, *s[1:])
                signals.end()


_INS = ["x_prompt", "x_sample", "c_prompt", "c_sample", "cache_kv_latent", "cache_k_rope", "page_table", "norm1_g",
        "norm2_g", "w_mod", "b_mod", "mla_w_in", "mla_g_q_a", "mla_g_kv_a", "mla_w_uq", "mla_g_q", "mla_w_uk",
        "mla_w_uv", "mla_g_k", "mla_w_o", "sg_w_in", "sg_b_in", "sg_g_v", "sg_w_s", "sg_b_s", "sg_w_out", "peer_w_q",
        "peer_sub_keys", "peer_u", "peer_v"]
_OUTS = {"y_prompt": (1, 256, D), "y_sample": (NT, 1, D), "new_kv_p": (1, 1, 256, KVR), "new_kr_p": (1, 1, 256, ROPE),
         "new_kv_s": (1, NT, 1, KVR), "new_kr_s": (1, NT, 1, ROPE), "new_v_p": (1, 1, P, SGH), "new_v_s": (1, NT, 1, SGH)}
_SCRATCH = {"modrows": ((2, 9, 6 * D), F32), "route_e": ((2, 64, TOPK), U32), "route_g": ((2, 64, TOPK), F32)}


def kernel(**inputs):
    import concourse.bacc as _bacc
    from concourse.bass_utils import run_bass_kernel_spmd as _run

    nc = _bacc.Bacc("TRN2", target_bir_lowering=False, num_devices=1)
    arrays, t = {}, {}

    def given(name, a):
        arrays[f"in_{name}"] = a
        t[name] = nc.dram_tensor(f"in_{name}", a.shape, mybir.dt.from_np(a.dtype), kind="ExternalInput").ap()

    for name in _INS:
        a = np.ascontiguousarray(inputs[name])
        if name == "cache_kv_latent":
            name, a = "cache_kv", a.reshape(-1, 8 * KVR)
        elif name == "cache_k_rope":
            name, a = "cache_kr", a.reshape(-1, 8 * ROPE)
        if name in ("peer_u", "peer_v"):
            for layer in range(2):
                given(f"{name}{layer}", a[layer])
            t[name] = [t[f"{name}{layer}"] for layer in range(2)]
        else:
            given(name, a)
    given("consts", constants())
    for name, shape in _OUTS.items():
        t[name] = nc.dram_tensor(f"out_{name}", shape, F32, kind="ExternalOutput").ap()
    for name, (shape, dt) in _SCRATCH.items():
        t[name] = nc.dram_tensor(name, shape, dt, kind="Internal").ap()
    program(nc, t)
    r = _run(nc, [arrays], core_ids=[0])
    return tuple(r.results[0][f"out_{name}"] for name in _OUTS)
```

```python
from contextlib import ExitStack

import numpy as np

import concourse.bass as bass
from concourse import mybir

F32 = mybir.dt.float32
U32 = mybir.dt.uint32
I32 = mybir.dt.int32
ALU = mybir.AluOpType
ACT = mybir.ActivationFunctionType
X = mybir.AxisListType.X

P = 128
D = 1024
KD = D // P
NT = 8
H = 8
NOPE, ROPE, HALF = 64, 32, 16
QK = NOPE + ROPE
QR, KVR = 256, 128
VD = 128
PAST, PAGE = 2048, 128
SM_SCALE = QK ** -0.5
SGH = 1536
SGG = SGH // P
PH, TOPK, NKEYS = 8, 16, 128
EPS = 1e-6
NEG = -1e30
GELU_C, GELU_K = 0.044715, 0.7978845608028654
RSQRT_MAGIC = float(0x5F3759DF)

A, B, S = 0, 1, 2
ROWS = (P, P, NT)
RING = 8
WRING = 3

CONST_PARTS = [("ident", 128), ("cmask", 128), ("cmask_t", 128), ("ones", 128), ("iota16", 16), ("pmod", 1),
               ("selt", 8), ("cos_p", 32), ("sin_p", 32), ("cos_c", 256), ("sin_c", 256), ("cos_q", 16),
               ("sin_q", 16), ("own_neg", 8), ("sel16", 128)]
CONST_AT, CONST_COLS = {}, 0
for _name, _n in CONST_PARTS:
    CONST_AT[_name] = (CONST_COLS, _n)
    CONST_COLS += _n


def constants():
    c = np.zeros((P, CONST_COLS), np.float32)

    def put(name, a):
        at, n = CONST_AT[name]
        a = np.asarray(a, np.float32)
        c[:a.shape[0], at:at + n] = a.reshape(a.shape[0], n)

    p = np.arange(P)
    put("ident", np.eye(P))
    put("cmask", np.where(p[None, :] <= p[:, None], 0.0, NEG))
    put("cmask_t", (p[:, None] <= p[None, :]).astype(np.float32))
    put("ones", np.ones((P, P)))
    put("iota16", np.tile(np.arange(16), (P, 1)))
    put("pmod", (p % 16)[:, None])
    put("selt", (p[:, None] // 16 == np.arange(8)[None, :]))
    put("sel16", (p[None, :] // 16 == np.arange(8)[:, None]))
    put("own_neg", np.where(np.eye(8) > 0, 0.0, NEG))
    inv = (np.float32(10000.0) ** (-np.arange(HALF, dtype=np.float32) * np.float32(2.0) / np.float32(ROPE)))

    def angles(pos):
        return (pos.astype(np.float32)[..., None] * inv).astype(np.float32)

    for name, pos in (("p", p[:, None] + P * np.arange(2)[None, :]),
                      ("c", (np.arange(2)[None, :, None] * 1024 + 8 * p[:, None, None] + np.arange(8)[None, None, :])),
                      ("q", np.full((NT, 1), PAST))):
        a = angles(pos)
        put("cos_" + name, np.cos(a))
        put("sin_" + name, np.sin(a))
    return c


def expert_steps():
    a0, b0, a1, b1 = ([(n, h) for h in range(PH)] for n in (0, 1, 3, 4))
    return a0 + b0 + a1 + b1[:3] + [(2, None)] + b1[3:] + [(5, None)]


STEPS = expert_steps()
SLOTS = [TOPK if h is not None else PH for _, h in STEPS]
SLOT0 = [sum(SLOTS[:p]) for p in range(len(STEPS) + 1)]
N_SLOTS = SLOT0[-1]
STEP_OF = [p for p, n in enumerate(SLOTS) for _ in range(n)]
LAG = 26
DIAG_AHEAD = 3
N_UNITS = N_SLOTS + LAG


def last_sum(n):
    return SLOT0[max(p for p, s in enumerate(STEPS) if s[0] == n) + 1] + LAG


def mods(layer, a, b):
    return [("mod", layer, j) for j in range(a, b)]


MODS_EARLY, MODS_MID = 8, 24
CACHES_EARLY = 2


def rope_before(b):
    return b not in (0, CACHES_EARLY)


def stretches():
    q = [[("query", n, h) for h in range(PH)] for n in range(6)]

    def woven(a, b):
        out, j = [], 0
        for i, st in enumerate(a):
            out.append(st)
            while (j + 1) * len(a) <= (i + 1) * len(b):
                out.append(b[j])
                j += 1
        return out

    start = ([("init",)] + mods(0, 0, 8) + [("norm", A, 0, 0), ("mla_in", A), ("attn", A), ("tables",), ("proj", A),
                                            ("norm", A, 0, 1), q[0][0]])
    sgu = lambda t: ([("norm", t, 1, 0)] + [("sgu_v", t, j) for j in range(6)] + [("sgu_vnorm", t)] +
                     [("sgu_u", t, j) for j in range(6)] + [("sgu_mix", t), ("sgu_out", t), ("norm", t, 1, 1)])
    caches = [("cache", b) for b in range(NT)]
    era0 = (woven(q[0][1:], mods(0, 20, 24) + mods(1, 0, MODS_EARLY)) +
            [("norm", B, 0, 0), ("mla_in", B), ("attn", B), ("proj", B), ("norm", B, 0, 1)] + q[1])
    n = CACHES_EARLY
    era1 = ([("peer_out", 0), ("norm", S, 0, 0), ("mla_in", S), ("cache_init",), ("sgu_init",)] +
            woven(sgu(A)[:-1], mods(1, MODS_EARLY, 20)) + sgu(A)[-1:] + woven(q[3], mods(1, 20, MODS_MID) + caches[:n]))
    era2 = [("peer_out", 1)] + woven(sgu(B), mods(1, MODS_MID, 24)) + woven(q[4], caches[n:])
    era3 = [("peer_out", 3), ("cache_out",), ("proj", S), ("norm", S, 0, 1), ("query_s", 2), ("topk_s", 2)]
    era4 = [("peer_out", 2), ("norm", S, 1, 0)] + [("sgu_s", j) for j in range(12)]
    era4 += [("sgu_s_mix",), ("sgu_out", S), ("norm", S, 1, 1), ("query_s", 5), ("topk_s", 5)]
    s0 = SLOT0[STEPS.index((2, None))]
    s1 = SLOT0[STEPS.index((5, None))]
    return [(0, start), (last_sum(0), era0), (last_sum(1), era1), (last_sum(3), era2), (s0 - 10, era3),
            (last_sum(2), []), (s1 - 10, era4), (last_sum(4), []), (N_UNITS, [("peer_out", 4)]), (N_UNITS, [("peer_out", 5)])]


FLOW = {"mod": "c 3", "norm": "5/4 3/4", "mla_in": "c c 6/0 c 0/6 12", "attn": "6/4 6/4 3/7", "proj": "c 3 c 3 c 3 c 3 3",
        "query": "c 4 6 5", "query_s": "c 3 c 3 c 3 c 3 c 3 c 3 c 3 c 3 3", "topk_s": "5 6", "cache_init": "5 3",
        "cache": "20/5 5/10 5/10 5/10 22/3 3/20 12", "sgu_v": "c 3", "sgu_u": "c 3", "sgu_s": "c 3",
        "sgu_vnorm": "10/2 5/13", "sgu_mix": "7/3 4/8", "sgu_s_mix": "10/2 8/10 4/10",
        "sgu_out": "c 3 c 3 c 3 c 3 c 3 c 3 3"}
SCHEDULE = [s for _, stages in stretches() for s in stages]
WHERE = {s: k for k, s in enumerate(SCHEDULE)}
V_SIDE, U_SIDE = 0, 1


def flow(k):
    return FLOW.get(SCHEDULE[k][0], "1").split()


def n_points(k):
    return len(flow(k)) - flow(k).count("c")


def place_units(side):
    at, k, done = {}, 0, 0
    for end, stages in stretches():
        points = []
        for _ in stages:
            weights = [float(f.split("/")[min(side, f.count("/"))]) for f in flow(k) if f != "c"]
            points += [((k, j), w) for j, w in enumerate(weights)]
            k += 1
        if points:
            total, run, first = sum(w for _, w in points), 0.0, done
            for key, w in points:
                run += w
                upto = end if key == points[-1][0] else min(end, first + int((end - first) * run / total + 0.5))
                at[key] = (done, upto)
                done = upto
        elif end > done:
            key = (k - 1, n_points(k - 1) - 1)
            at[key] = (at[key][0], end)
            done = end
    return at


SIDES = (place_units(V_SIDE), place_units(U_SIDE))
UNITS = SIDES[U_SIDE]
AHEAD = [SIDES[V_SIDE][key][1] - SIDES[U_SIDE][key][1] for key in UNITS]
assert max(AHEAD) <= LAG - DIAG_AHEAD - TOPK - 1 and min(AHEAD) > -RING + 1, (max(AHEAD), min(AHEAD))
EARLY = {}
_early = mods(0, 8, 20)
for _s, _n in ((("norm", A, 0, 0), (2, 1)), (("mla_in", A), (2, 1, 2)), (("attn", A), (2, 2, 0))):
    for _j, _m in enumerate(_n):
        EARLY[WHERE[_s], _j] = _early[:_m]
        _early = _early[_m:]
assert not _early


def labels(step):
    kind, tile = step[0], step[1] if len(step) > 1 else None
    if kind == "init":
        return ["cT"], ["silu", "siluT"], ["tanh"]
    if kind == "tables":
        return ["keysT", "ukT"], ["keysT", "ukT"], []
    if kind == "norm":
        rep = ["rep"] if tile == S and step[3] else []
        return ["hT0", "hT1"] + rep, ["h"], ["hT0", "hT1"] + rep
    if kind == "mla_in":
        return ["z", "cT", "qk"], ["c", "kr", "qk"], ["z", "cT", "qk", "sq"]
    if kind == "attn":
        kt = range(1 + tile)
        pe, dve, act = ["qT0", "qT1", "kT0", "kT1"], ["qT0", "qT1"], ["kT0", "kT1"]
        for f in "01":
            pe += ["s" + f, *[f"pT{f}{q}" for q in kt], "ol" + f]
            dve += ["max" + f, "p" + f, "ol" + f]
            act += ["exp" + f, *[f"pT{f}{q}" for q in kt]]
        return pe + ["oT"], dve + ["oT"], act
    if kind == "cache_init":
        return (["qgT", "qabs", "qrT", "pages"], ["qg", "qr", "pages_f", "qgT", "qabs", "qpad", "pages"], [])
    if kind == "cache":
        own = [] if rope_before(tile) else ["rope", "krsq"]
        after_it = ["rope", "krsq"] if tile + 1 < NT and rope_before(tile + 1) else []
        return (["krT", "cT0", "cT1", "kn0", "kn1", "cT2", "kn2", "kn3", "cT3", "kn4", "kn5", "kn6", "kn7",
                 "maxT", "maxb", "pv"],
                [*own, *[f"ssn{i}" for i in range(8)], "max", "diag", "shift", "sum",
                 *[f"{n}+" for n in after_it[:1]], "ol", *[f"{n}+" for n in after_it[1:]]],
                [*own[1:], "krT", "cT0", "cT1", "sq0", "sq1", "cT2", "sq2", "sq3", "cT3", "sq4", "sq5", "sq6", "sq7",
                 "exp", *[f"{n}+" for n in after_it[1:]]])
    if kind == "cache_out":
        return ["oT"], ["oT"], []
    if kind == "proj":
        return ["w0", "w1", "w2", "w3"], ["x"], []
    if kind == "query":
        return ["q", "s"], ["top", "topk"], ["q", "s", "exp"]
    if kind == "query_s":
        return ([f"q{h}" for h in range(PH)] + ["qT", "s"], [], [f"q{h}" for h in range(PH)] + ["qT", "s"])
    if kind == "topk_s":
        return [], ["top", "topk"], ["exp"]
    if kind == "sgu_init":
        return ["wT0", "wT1", "wT2"], ["wT0", "wT1", "wT2"], []
    if kind == "sgu_v":
        return ["v"], [], ["v"]
    if kind == "sgu_vnorm":
        return [], ["poly", "v"], ["tanh"]
    if kind == "sgu_u":
        return ["u"], [], ["u"]
    if kind == "sgu_mix":
        return ["s"], ["poly", "gated"], ["tanh"]
    if kind == "sgu_s":
        return ["z"], [], ["z"]
    if kind == "sgu_s_mix":
        return ["gT"], ["poly", "v", "gated", "gT"], ["tanh"]
    if kind == "sgu_out":
        return [f"w{i}" for i in range(6)], ["x"], []
    if kind == "peer_out":
        return [], ["x"], []
    return [], [], []


PE, DVE, ACTE = 0, 1, 2


def chunk_labels(step):
    return {"mla_in": ["z", "z", "qk"], "proj": ["w0", "w1", "w2", "w3"], "query": ["q"],
            "query_s": [f"q{h}" for h in range(PH)], "sgu_v": ["v"], "sgu_u": ["u"], "sgu_s": ["z"],
            "sgu_out": [f"w{i}" for i in range(6)]}[step[0]]


BASE, CHUNKS, MODS, MODS0 = [], [], [], []
_b = [0, 0, 0]
for _k, _s in enumerate(SCHEDULE):
    BASE.append(tuple(_b))
    MODS0.append(len(MODS))
    _b = [n + len(ls) for n, ls in zip(_b, labels(_s))]
    _i = _j = 0
    for _f in flow(_k):
        if _f == "c":
            CHUNKS.append((_s, _i))
            _i += 1
            if _s[0] == "mod":
                MODS.append(_s)
        else:
            for _m in EARLY.get((_k, _j), ()):
                CHUNKS.append((_m, 0))
                MODS.append(_m)
            _j += 1
CHUNK_AT = {c: i for i, c in enumerate(CHUNKS)}
NORMS = [k for k, s in enumerate(SCHEDULE) if s[0] == "norm"]
PQ_USERS = ("attn", "cache_init", "cache", "sgu_init", "sgu_mix")
GAINS = [k for k, s in enumerate(SCHEDULE) if s[0] in ("norm", "proj", "sgu_out", "peer_out")]
ARENA = 7680
N_ONCE = 9
for _p, (_n, _h) in enumerate(STEPS):
    _q = WHERE[("topk_s", _n) if _h is None else ("query", _n, _h)]
    assert UNITS[_q, n_points(_q) - 1][0] <= SLOT0[_p], (_n, _h)
for _n in (0, 1, 2, 3, 4, 5):
    assert UNITS[WHERE[("peer_out", _n)], 0][0] >= last_sum(_n) or _n >= 4, _n
for _n in (0, 1, 3):
    assert UNITS[WHERE[("peer_out", _n)], 0][0] == last_sum(_n), _n


def reached(e, k, name):
    return BASE[k][e] + labels(SCHEDULE[k])[e].index(name) + 1


def program(nc, t):
    with ExitStack() as ctx:
        def sb(name, shape, dt=F32):
            return ctx.enter_context(nc.sbuf_tensor(name, shape, dt))

        def psum(name, shape):
            return ctx.enter_context(nc.psum_tensor(name, shape, F32))

        def sem(name):
            return ctx.enter_context(nc.semaphore(name))

        cst = sb("cst", [P, CONST_COLS])

        def const(name, rows=P):
            at, n = CONST_AT[name]
            return cst[0:rows, at:at + n]

        ident, ones = const("ident"), const("ones")
        x = [sb(f"x{i}", [P, D]) for i in range(3)]
        hT = sb("hT", [P, KD, P])
        h_rep = sb("h_rep", [P, D])
        uring, vring = sb("uring", [P, RING, D]), sb("vring", [P, RING, D])
        wring = sb("wring", [P, WRING, 2048])
        modg, mods = sb("modg", [P, D]), sb("mods", [P, D])
        diag = sb("diag", [P, RING, P])
        expert = [sb(f"expert{i}", [P, PH, TOPK], U32) for i in range(2)]
        gate = [sb(f"gate{i}", [P, PH, TOPK]) for i in range(2)]
        expert_s, gate_s = sb("expert_s", [P, PH], U32), sb("gate_s", [P, PH])
        top_s, topi_s = sb("top_s", [64, TOPK]), sb("topi_s", [64, TOPK], U32)
        dots, wts = sb("dots", [P, 2, TOPK]), sb("wts", [P, 2, TOPK])
        ew = sb("ew", [P, 3, TOPK])
        keysT = sb("keysT", [P, 4, NKEYS])
        siluT = sb("siluT", [P, KD, 9])
        gbc = sb("gbc", [P, QR + KVR + 2 * QK])
        gqa, gkva, gqk = gbc[:, 0:QR], gbc[:, QR:QR + KVR], gbc[:, QR + KVR:QR + KVR + 2 * QK]
        w_uk, w_uv, w_ukT = sb("w_uk", [P, H * NOPE]), sb("w_uv", [P, H * VD]), sb("w_ukT", [P, 4, P])
        mrow, mbg = sb("mrow", [9, 2, 256]), sb("mbg", [9, 2, 2, 256])
        scr, rs = sb("scr", [P, 64]), sb("rs", [P, 48])
        qs = sb("qs", [P, 2, P])
        sc, work = sb("sc", [P, 2, NKEYS]), sb("work", [P, 256])
        t1, ti = sb("t1", [P, 2, TOPK]), sb("ti", [P, 2, TOPK], U32)
        cand, hot = sb("cand", [P, TOPK * TOPK]), sb("hot", [P, TOPK, TOPK])
        ctop, ci, cu = sb("ctop", [P, TOPK]), sb("ci", [P, TOPK], U32), sb("cu", [P, 2, TOPK], U32)
        cf, ef = sb("cf", [P, 4, TOPK]), sb("ef", [P, 2, TOPK])
        eg = sb("eg", [P, TOPK + 4])
        kv, kr = sb("kv", [P, 16, KVR]), sb("kr", [P, 2, 16, ROPE])
        ptab, page_rows = sb("ptab", [NT, 16], I32), sb("page_rows", [P, 16], U32)
        ptab_f = sb("ptab_f", [NT, 16])
        ckv, krt = [sb(f"ckv{i}", [P, KVR]) for i in range(3)], [sb(f"krt{i}", [P, ROPE]) for i in range(3)]
        qabs, qpad = sb("qabs", [P, NT, H]), sb("qpad", [P, NT, 4, H])
        olS, scores, own = sb("olS", [P, H, NT]), sb("scores", [P, 17, H]), sb("own", [NT, H])
        w00 = sb("w00", [NT, 2, SGG])

        arena = sb("arena", [P, ARENA])
        taken = [0]

        def region(at):
            taken[0] = at

        def part(n):
            taken[0] += n
            assert taken[0] <= ARENA, taken[0]
            return arena[:, taken[0] - n:taken[0]]

        region(0)
        z_, cT_, qk_ = part(416), part(3 * P), part(2 * H * QK)
        kT = [part(H * P) for _ in range(2)]
        qT = part(H * P)
        att, prob = part(1024), part(1024)
        sq_, rt_ = arena[:, taken[0] - 2048:taken[0] - 512], qT
        ol, oT = qk_[:, 0:H * P], qT
        region(0)
        wcT = part(SGG * P)
        rows = part(SGH)
        sv, su, stmp = part(SGH), part(SGH), part(SGH)
        region(2 * SGH)
        krr, krT, cTc, knsq = part(16 * ROPE), part(4 * P), part(2 * 4 * P), part(2 * 1024)
        ssn, rkk, pr = part(16 * H), part(16 * H), part(17 * H)
        rope_t, krsq = knsq[:, 0:1024], knsq[:, 1024:1536]
        oTs = krr[:, 0:H * NT]
        region(2 * SGH)
        z_s, cT_s, qk_s, sq_s, rt_s = part(416), part(24), part(2 * H * QK), part(2 * H * QK), part(1024)
        q_s = arena[:, 2 * SGH:2 * SGH + 256 * PH]
        h_tok = [sb("h0", [P, D]), sb("h1", [P, D]), arena[:, ARENA - D:ARENA]]

        yacc, pp, pq = psum("yacc", [P, 2, 512]), psum("pp", [P, 2, 512]), psum("pq", [P, 2, 512])
        ps = [psum("ps0", [P, 512]), psum("ps1", [P, 512])]

        stage_done = [sem("pe_stage"), sem("dve_stage"), sem("act_stage")]
        mod_done = [sem("pe_mod"), sem("dve_mod")]
        dve_chain = sem("dve_chain")
        act_chain = sem("act_chain")
        in_first, in_x, in_once, pages_in = sem("in_first"), sem("in_x"), sem("in_once"), sem("pages_in")
        w_land = [sem(f"w_land{i}") for i in range(WRING)]
        u_land, v_land = [sem(f"u_land{i}") for i in range(RING)], [sem(f"v_land{i}") for i in range(RING)]
        u_used, v_used = sem("u_used"), sem("v_used")
        poly_ready, tanh_ready, w_ready = sem("poly_ready"), sem("tanh_ready"), sem("w_ready")
        diag_ready = sem("diag_ready")
        mbias_in, mrow_out = [sem("mbias_in0"), sem("mbias_in1")], [sem("mrow_out0"), sem("mrow_out1")]
        g_land, s_land = sem("g_land"), sem("s_land")
        out_done, v_out = sem("out_done"), sem("v_out")
        route_out, route_in = sem("route_out"), sem("route_in")
        sgu_in, gv_in, w00_in, kv_in = sem("sgu_in"), sem("gv_in"), sem("w00_in"), sem("kv_in")
        kr_in = [sem("kr_in0"), sem("kr_in1")]

        def after(eng, e, k, name):
            eng.wait_ge(stage_done[e], reached(e, k, name))

        def begin(eng, k):
            kind, j = SCHEDULE[k][0], k - 1
            while SCHEDULE[j][0] == "mod":
                j -= 1
            if SCHEDULE[j][0] == "query":
                after(eng, ACTE, j, "s")
                for e in (PE, DVE):
                    eng.wait_ge(stage_done[e], BASE[j][e])
            else:
                if not (kind in ("sgu_v", "sgu_u", "sgu_s") and SCHEDULE[j][0] == kind):
                    j = k
                for e in (PE, DVE, ACTE):
                    if BASE[j][e]:
                        eng.wait_ge(stage_done[e], BASE[j][e])
            if kind in PQ_USERS and MODS0[k]:
                eng.wait_ge(mod_done[DVE], MODS0[k])

        class Signals:

            def __init__(self, eng, e):
                self.eng, self.e, self.k, self.n = eng, e, 0, 0

            def start(self, k):
                self.k, self.n = k, 0

            def __call__(self, ins, name):
                assert labels(SCHEDULE[self.k])[self.e][self.n] == name, (SCHEDULE[self.k], name)
                self.n += 1
                ins.then_inc(stage_done[self.e], 1)

            def end(self):
                assert self.n == len(labels(SCHEDULE[self.k])[self.e]), (SCHEDULE[self.k], self.e, self.n)

        def mod_bank(i):
            return yacc[:, i % 2] if i < MODS0[WHERE[("query", 0, 0)]] else pq[:, i % 2]

        points_seen = {}

        def early_or_units(k, j, e, mod, v_unit, u_unit):
            assert points_seen.get((e, k), 0) == j, (SCHEDULE[k], e, j)
            points_seen[e, k] = j + 1
            for m in EARLY.get((k, j), ()):
                mod(k, *m[1:])
            v, u = (range(*side[k, j]) for side in SIDES)
            for g in range(min(v.start, u.start), max(v.stop, u.stop)):
                if g in v:
                    v_unit(g)
                if g in u:
                    u_unit(g)

        def shape_of(tile, prompt, sample):
            return sample if tile == S else prompt

        block = ctx.enter_context(nc.Block())

        @block.sync
        def _(sp):
            def bcast(ap, r):
                return ap.to_broadcast([r, ap.shape[-1]])

            def mod_row(tile, layer, j):
                if tile == S:
                    return t["modrows"][layer, 1:9, j * D:(j + 1) * D]
                return bcast(t["modrows"][layer, 0:1, j * D:(j + 1) * D], P)

            first = ((cst[:, :], t["consts"]), (h_rep[0:1, :], t["c_prompt"]), (h_rep[1:9, :], t["c_sample"]))
            once = ((x[B][:, :], t["x_prompt"][0, P:2 * P, :]),
                    (x[S][0:NT, :], t["x_sample"][:, 0, :]),
                    (gqa, bcast(t["mla_g_q_a"], P)), (gkva, bcast(t["mla_g_kv_a"], P)),
                    (gqk[:, 0:QK], bcast(t["mla_g_q"], P)), (gqk[:, QK:2 * QK], bcast(t["mla_g_k"], P)),
                    (w_uk[:, :], t["mla_w_uk"][0].rearrange("c h d -> c (h d)")),
                    (w_uv[:, :], t["mla_w_uv"][0].rearrange("c h d -> c (h d)")),
                    (diag[:, 0:4, :], t["peer_sub_keys"].rearrange("l s n k -> n (l s) k")))
            assert len(once) == N_ONCE
            for dst, src in first:
                sp.dma_start(dst, src).then_inc(in_first, 16)

            def load_once():
                for dst, src in once:
                    sp.dma_start(dst, src).then_inc(in_once, 16)

            for half in range(2):
                sp.dma_start(ptab[:, 8 * half:8 * half + 8],
                             t["page_table"][:, 8 * half:8 * half + 8].rearrange("b g -> g b"),
                             allow_slow_non_contiguous=True).then_inc(pages_in, 16)

            def chunk_source(s, i):

                def columns(w, j):
                    return w[:, 256 * j:256 * j + 256].rearrange("(k p) n -> p k n", p=P)

                def rows_of(w, i, n):
                    return w[n * i:n * i + n, :].rearrange("(k p) n -> p k n", p=P)

                if s[0] == "mod":
                    return columns(t["w_mod"][s[1]], s[2])
                if s[0] == "mla_in":
                    return rows_of(t["mla_w_in"][0], i, 512) if i < 2 else rows_of(t["mla_w_uq"][0], 0, QR)
                if s[0] == "proj":
                    return rows_of(t["mla_w_o"][0], i, 256)
                if s[0] == "sgu_out":
                    return rows_of(t["sg_w_out"][0], i, 256)
                if s[0] in ("query", "query_s"):
                    return columns(t["peer_w_q"][s[1] // 3], s[2] if s[0] == "query" else i)
                return columns(t["sg_w_in"][0], {"sgu_v": 6 + s[-1], "sgu_u": s[-1], "sgu_s": s[-1]}[s[0]])

            loaded = [0]

            def load_chunks(until):
                while loaded[0] < min(until, len(CHUNKS)):
                    n = loaded[0]
                    src = chunk_source(*CHUNKS[n])
                    if n >= WRING:
                        st, i = CHUNKS[n - WRING]
                        if st[0] == "mod":
                            sp.wait_ge(mod_done[PE], MODS.index(st) + 1)
                        else:
                            after(sp, PE, WHERE[st], chunk_labels(st)[i])
                    kk, w = src.shape[1], src.shape[2]
                    sp.dma_start(wring[:, n % WRING, 0:kk * w].rearrange("p (k n) -> p k n", k=kk), src)\
                      .then_inc(w_land[n % WRING], 16)
                    loaded[0] += 1

            def load_mod_bias(i):
                _, l, j = MODS[i]
                if i >= 2:
                    sp.wait_ge(mod_done[DVE], i - 1)
                g = t["norm1_g"] if j < 12 else t["norm2_g"]
                at = 256 * (j % 4)
                sp.dma_start(mbg[:, i % 2, 0, :], bcast(t["b_mod"][l:l + 1, 256 * j:256 * j + 256], 9))\
                  .then_inc(mbias_in[i % 2], 16)
                sp.dma_start(mbg[:, i % 2, 1, :], bcast(g[l:l + 1, at:at + 256], 9)).then_inc(mbias_in[i % 2], 16)

            stored = [0]

            def store_mod(i):
                _, l, j = MODS[i]
                sp.wait_ge(mod_done[DVE], i + 1)
                sp.dma_start(t["modrows"][l, :, 256 * j:256 * j + 256], mrow[:, i % 2, :]).then_inc(mrow_out[i % 2], 16)
                if i + 2 < len(MODS):
                    load_mod_bias(i + 2)
                stored[0] += 1

            def rows_needed(k):
                s = SCHEDULE[k]
                if s[0] == "norm":
                    return s[1], s[2], 3 * s[3] + 1, 3 * s[3]
                if s[0] == "peer_out":
                    return s[1] % 3, s[1] // 3, 5, None
                return s[1], int(s[0] == "sgu_out"), 2, None

            def in_dram(layer, row):
                n = MODS.index(("mod", layer, 4 * row + 3)) + 1
                return n <= stored[0], n

            def wait_in_dram(n):
                for q in range(2):
                    sp.wait_ge(mrow_out[q], 16 * ((n + 1 - q) // 2))

            next_g, next_s = [0], [0]

            def load_gains(k):
                i = next_g[0]
                if i < len(GAINS) and (i == 0 or GAINS[i - 1] < k):
                    tile, layer, row, _ = rows_needed(GAINS[i])
                    ready, n = in_dram(layer, row)
                    if ready:
                        if i:
                            j = GAINS[i - 1]
                            after(sp, DVE, j, "h" if SCHEDULE[j][0] == "norm" else "x")
                        wait_in_dram(n)
                        sp.dma_start(modg[0:ROWS[tile], :], mod_row(tile, layer, row)).then_inc(g_land, 16)
                        next_g[0] += 1
                i = next_s[0]
                if i < len(NORMS) and (i == 0 or NORMS[i - 1] < k):
                    tile, layer, _, row = rows_needed(NORMS[i])
                    ready, n = in_dram(layer, row)
                    if ready:
                        if i:
                            after(sp, DVE, NORMS[i - 1], "h")
                        wait_in_dram(n)
                        sp.dma_start(mods[0:ROWS[tile], :], mod_row(tile, layer, row)).then_inc(s_land, 16)
                        next_s[0] += 1

            outs = [0]

            def store(dst, src):
                sp.dma_start(dst, src).then_inc(out_done, 16)
                outs[0] += 1

            load_mod_bias(0)
            load_chunks(2)
            sp.dma_start(x[A][:, :], t["x_prompt"][0, 0:P, :]).then_inc(in_x, 16)
            load_mod_bias(1)
            for k, s in enumerate(SCHEDULE):
                kind, tile = s[0], s[1] if len(s) > 1 else None
                if kind == "sgu_v" and s[2] == 0:
                    begin(sp, k)
                    sp.dma_start(su, bcast(t["sg_g_v"], P)).then_inc(gv_in, 16)
                if s[0] in ("mod", "proj", "attn"):
                    while stored[0] < MODS0[k]:
                        store_mod(stored[0])
                load_gains(k)
                i = j = 0
                for f in flow(k):
                    if f == "c":
                        load_chunks(CHUNK_AT[s, i] + WRING)
                        i += 1
                    else:
                        for m in EARLY.get((k, j), ()):
                            load_chunks(CHUNK_AT[m, 0] + WRING)
                            if MODS.index(m) > stored[0]:
                                store_mod(stored[0])
                        j += 1
                if kind == "mod":
                    store_mod(MODS.index(s))
                if s == ("norm", A, 0, 0):
                    load_once()
                load_gains(k)
                if kind in ("norm", "proj", "sgu_out", "peer_out"):
                    assert next_g[0] > GAINS.index(k) and (kind != "norm" or next_s[0] > NORMS.index(k)), s
                if kind == "peer_out" and s[1] // 3 == 1:
                    tile = s[1] % 3
                    after(sp, DVE, k, "x")
                    store(t["y_sample"][:, 0, :] if tile == S else t["y_prompt"][0, P * tile:P * tile + P, :],
                          x[tile][0:ROWS[tile], :])
                elif kind == "mla_in":
                    after(sp, DVE, k, "c")
                    at = slice(P * tile, P * tile + P)
                    store(t["new_kv_s"][0, :, 0, :] if tile == S else t["new_kv_p"][0, 0, at, :],
                          ckv[tile][0:ROWS[tile], :])
                    store(t["new_kr_s"][0, :, 0, :] if tile == S else t["new_kr_p"][0, 0, at, :],
                          krt[tile][0:ROWS[tile], :])
                elif kind == "sgu_init":
                    begin(sp, k)
                    sp.dma_start(sv.rearrange("p (g s) -> p g s", g=SGG), t["sg_w_s"][0].rearrange("g t s -> t g s"))\
                      .then_inc(sgu_in, 16)
                    sp.dma_start(rows[0:1, :], t["sg_b_in"][:, SGH:2 * SGH]).then_inc(sgu_in, 16)
                    sp.dma_start(rows[32:33, :], t["sg_b_in"][:, 0:SGH]).then_inc(sgu_in, 16)
                    sp.dma_start(rows[64:65, :], t["sg_b_s"].rearrange("l g t -> l (g t)")).then_inc(sgu_in, 16)
                    for i, w in enumerate((t["sg_w_s"][0, :, 0, 0:1], t["sg_b_s"][0, :, 0:1])):
                        sp.dma_start(w00[:, i, :], bcast(w.rearrange("g o -> o g"), NT),
                                     allow_slow_non_contiguous=True).then_inc(w00_in, 16)
                elif kind == "sgu_vnorm":
                    if tile == B:
                        after(sp, DVE, k, "v")
                        sp.dma_start(t["new_v_p"][0, 0], sv).then_inc(v_out, 16)
                elif kind == "sgu_s_mix":
                    begin(sp, k)
                    sp.dma_start(wcT[0:NT, :], bcast(t["sg_g_v"], NT)).then_inc(gv_in, 16)
                    after(sp, DVE, k, "v")
                    sp.dma_start(t["new_v_s"][0, :, 0, :], sv[0:NT, :]).then_inc(v_out, 16)
                elif kind == "topk_s":
                    i = s[1] // 3
                    after(sp, DVE, k, "topk")
                    sp.dma_start(t["route_e"][i], topi_s[:, :]).then_inc(route_out, 16)
                    sp.dma_start(t["route_g"][i], top_s[:, :]).then_inc(route_out, 16)
                    sp.wait_ge(route_out, 32 * (i + 1))
                    for b in range(NT):
                        for dst, src in ((expert_s, t["route_e"]), (gate_s, t["route_g"])):
                            sp.dma_start(dst[16 * b:16 * b + 16, :], src[i][8 * b:8 * b + 8, :].rearrange("h k -> k h"),
                                         allow_slow_non_contiguous=True).then_inc(route_in, 16)
            sp.wait_ge(out_done, 16 * outs[0])
            sp.wait_ge(v_out, 32)

        @block.gpsimd
        def _(pool):
            def gather(slot, ring, table, used, land):
                n, h = STEPS[STEP_OF[slot]]
                i = slot - SLOT0[STEP_OF[slot]]
                if slot >= RING:
                    pool.wait_ge(used, slot - RING + 1)
                idx = expert_s[:, i:i + 1] if h is None else expert[n % 3][:, h, i:i + 1]
                pool.indirect_dma_start(ring[:, slot % RING, :], None, table[n // 3],
                                        bass.IndirectOffsetOnAxis(ap=idx, axis=0)).then_inc(land[slot % RING], 16)

            def gather_cache(b, dst, src, land):
                for half in range(2):
                    idx = page_rows[:, 8 * half + b:8 * half + b + 1]
                    pool.indirect_dma_start(dst[:, 8 * half:8 * half + 8, :].rearrange("p r c -> p (r c)"), None, src,
                                            bass.IndirectOffsetOnAxis(ap=idx, axis=0)).then_inc(land, 16)

            kv_at, kr_at = {}, {}
            for b in range(NT):
                k, last = WHERE[("cache", b)], WHERE[("cache", b - 1) if b else ("cache_init",)]
                done = UNITS[last, n_points(last) - 1][0]
                kv_at.setdefault(min(UNITS[k, 0][0], done + 4), []).append(b)
                kr_at.setdefault(min(UNITS[last, 0][0] + 3, UNITS[k, 0][0]) if b else done, []).append(b)
            for g in range(N_UNITS):
                for b in kr_at.get(g, ()):
                    if b == 0:
                        after(pool, DVE, WHERE[("cache_init",)], "pages")
                    elif b >= 2:
                        k = WHERE[("cache", b - 2 if rope_before(b - 1) else b - 1)]
                        after(pool, DVE, k, "krsq+" if rope_before(b - 1) else "krsq")
                    gather_cache(b, kr[:, b % 2], t["cache_kr"], kr_in[b % 2])
                for b in kv_at.get(g, ()):
                    if b:
                        after(pool, PE, WHERE[("cache", b - 1)], "pv")
                    gather_cache(b, kv, t["cache_kv"], kv_in)
                if g < N_SLOTS:
                    p = STEP_OF[g]
                    n, h = STEPS[p]
                    if g == SLOT0[p]:
                        if h is None:
                            pool.wait_ge(route_in, 16 * 2 * NT * (n // 3 + 1))
                        else:
                            after(pool, DVE, WHERE[("query", n, h)], "topk")
                    gather(g, uring, t["peer_u"], u_used, u_land)
                if g >= LAG:
                    gather(g - LAG, vring, t["peer_v"], v_used, v_land)

        @block.tensor
        def _(pe):
            signal = Signals(pe, PE)

            def chunk(k, i, kk, width=2048):
                n = CHUNK_AT[SCHEDULE[k], i]
                pe.wait_ge(w_land[n % WRING], 16 * (n // WRING + 1))
                return wring[:, n % WRING, 0:width].rearrange("p (k n) -> p k n", k=kk)

            def transposes(out, tiles, r):
                for i, a in enumerate(tiles):
                    last = pe.transpose(out[0:a.shape[-1], r * i:r * i + r], a, ident[0:r, 0:r])
                return last

            def init(k):
                pe.wait_ge(in_first, 48)
                after(pe, DVE, k, "silu")
                for c in range(KD):
                    last = pe.transpose(ps[0][:, 16 * c:16 * c + 9], h_rep[0:9, P * c:P * c + P], ident[0:9, 0:9])
                signal(last, "cT")

            def tables(k):
                begin(pe, k)
                pe.wait_ge(in_once, 16 * N_ONCE)
                signal(transposes(ps[1], [diag[:, c, :] for c in range(4)], P), "keysT")
                signal(transposes(pp[:, 0], [w_uk[:, P * c:P * c + P] for c in range(4)], P), "ukT")

            def mod(k, l, j):
                i = MODS.index(("mod", l, j))
                users = [u for u in range(k) if SCHEDULE[u][0] in ("init", *PQ_USERS)]
                if SCHEDULE[k][0] == "mod":
                    for e in (PE, DVE, ACTE):
                        pe.wait_ge(stage_done[e], BASE[users[-1] + 1][e])
                if i >= 2:
                    pe.wait_ge(mod_done[DVE], i - 1)
                n = CHUNK_AT[("mod", l, j), 0]
                pe.wait_ge(w_land[n % WRING], 16 * (n // WRING + 1))
                w, out = wring[:, n % WRING, :].rearrange("p (k n) -> p k n", k=8), mod_bank(i)
                for c in range(KD):
                    last = pe.matmul(out[0:9, 0:256], siluT[:, c, :], w[:, c, :], start=c == 0, stop=c == KD - 1)
                last.then_inc(mod_done[PE], 1)

            def norm(k, tile, layer, second):
                point(k, 0)
                begin(pe, k)
                after(pe, DVE, k, "h")
                r, h = ROWS[tile], h_tok[tile]
                for q in range(2):
                    signal(transposes(ps[q], [h[0:r, P * c:P * c + P] for c in range(4 * q, 4 * q + 4)], r), f"hT{q}")
                if tile == S and second:
                    for q in range(2):
                        last = pe.matmul(pp[:, q], const("sel16", NT), h[0:NT, 512 * q:512 * q + 512], start=True, stop=True)
                    signal(last, "rep")

            def mla_in(k, tile):
                begin(pe, k)
                r = ROWS[tile]
                z, cT = shape_of(tile, z_, z_s), shape_of(tile, cT_, cT_s)
                for c in range(KD):
                    w = chunk(k, c // 4, 4, 4 * 416)
                    last = pe.matmul(ps[0][0:r, 0:416], hT[:, c, 0:r], w[:, c % 4, :], start=c == 0, stop=c == KD - 1)
                signal(last, "z")
                point(k, 0)
                after(pe, DVE, k, "c")
                signal(transposes(ps[1], [z[0:r, 0:P], z[0:r, P:2 * P], ckv[tile][0:r, :]], r), "cT")
                after(pe, ACTE, k, "cT")
                after(pe, ACTE, k, "z")
                w = chunk(k, 2, 2, 2 * H * QK)
                for out, a, b in ((pp[0:r, 0, 0:480], 0, 480), (pp[0:r, 1, 0:288], 480, 768)):
                    for c in range(2):
                        pe.matmul(out, cT[:, r * c:r * c + r], w[:, c, a:b], start=c == 0, stop=c == 1)
                signal(pe.matmul(ps[0][0:r, :], cT[:, 2 * r:3 * r], w_uk[:, :], start=True, stop=True), "qk")
                point(k, 1)

            def attn(k, tile):
                begin(pe, k)
                kt = 1 + tile
                q3 = qk_.rearrange("p (i h d) -> p i h d", i=2, h=H)
                for i, names in enumerate((("qT0", "qT1"), ("kT0", "kT1"))):
                    for f in range(2):
                        out = ps[f] if i == 0 else pq[:, f]
                        signal(transposes(out, [q3[:, i, h, :] for h in range(4 * f, 4 * f + 4)], P), names[f])
                for f in range(2):
                    if f == 0:
                        after(pe, DVE, k, "qT1")
                        after(pe, ACTE, k, "kT1")
                    else:
                        after(pe, DVE, k, "max0")
                    for i in range(4):
                        h = 4 * f + i
                        for q in range(kt):
                            at = P * (kt * i + q)
                            last = pe.matmul(pp[:, at // 512, at % 512:at % 512 + P], qT[0:QK, P * h:P * h + P],
                                             kT[q][0:QK, P * h:P * h + P], start=True, stop=True)
                    signal(last, f"s{f}")
                    point(k, f)
                    after(pe, DVE, k, f"p{f}")
                    for q in range(kt):
                        signal(transposes(ps[q], [prob[:, P * (kt * i + q):P * (kt * i + q) + P] for i in range(4)], P),
                               f"pT{f}{q}")
                    for q in range(kt):
                        after(pe, ACTE, k, f"pT{f}{q}")
                        last = pe.matmul(pq[:, f], ckv[q][:, :], att[:, 512 * q:512 * q + 512], start=q == 0, stop=q == kt - 1)
                    signal(last, f"ol{f}")
                after(pe, DVE, k, "ol1")
                for h in range(H):
                    last = pe.matmul(ps[h // 4][:, P * (h % 4):P * (h % 4) + P], w_uv[:, VD * h:VD * h + VD],
                                     ol[:, P * h:P * h + P], start=True, stop=True)
                signal(last, "oT")

            def projection(k, tile, lhs, n):
                begin(pe, k)
                r = ROWS[tile]
                for i in range(n):
                    w = chunk(k, i, 2)
                    for c in range(2):
                        g = 2 * i + c
                        for q in range(2):
                            last = pe.matmul(pp[0:r, q], lhs[:, r * g:r * g + r], w[:, c, 512 * q:512 * q + 512],
                                             start=g == 0, stop=g == 2 * n - 1)
                    signal(last, f"w{i}")
                    point(k, i)

            def proj(k, tile):
                projection(k, tile, oTs if tile == S else oT, 4)

            def sgu_out(k, tile):
                projection(k, tile, su, 6)

            def query(k, n, h):
                begin(pe, k)
                w = chunk(k, 0, 8)
                for side in range(2):
                    for c in range(KD):
                        last = pe.matmul(ps[0][:, P * side:P * side + P], w[:, c, P * side:P * side + P], hT[:, c, :],
                                         start=c == 0, stop=c == KD - 1)
                signal(last, "q")
                point(k, 0)
                after(pe, ACTE, k, "q")
                for side in range(2):
                    last = pe.matmul(ps[1][:, P * side:P * side + P], qs[:, side, :], keysT[:, 2 * (n // 3) + side, :],
                                     start=True, stop=True)
                signal(last, "s")
                point(k, 1)

            def query_s(k, n):
                begin(pe, k)
                for h in range(PH):
                    w, out = chunk(k, h, 8), ps[h % 2][0:NT, 0:256]
                    if h >= 2:
                        after(pe, ACTE, k, f"q{h - 2}")
                    for c in range(KD):
                        last = pe.matmul(out, hT[:, c, 0:NT], w[:, c, :], start=c == 0, stop=c == KD - 1)
                    signal(last, f"q{h}")
                    point(k, h)
                after(pe, ACTE, k, f"q{PH - 1}")
                signal(transposes(ps[0], [q_s[0:NT, 256 * h + P * side:256 * h + P * side + P]
                                          for side in range(2) for h in range(PH)], NT), "qT")
                after(pe, ACTE, k, "qT")
                for side in range(2):
                    last = pe.matmul(ps[1][0:64, P * side:P * side + P], qs[:, side, 0:64],
                                     keysT[:, 2 * (n // 3) + side, :], start=True, stop=True)
                signal(last, "s")

            def cache_init(k):
                begin(pe, k)
                point(k, 0)
                after(pe, DVE, k, "qg")
                signal(transposes(ps[0], [sq_s[0:NT, P * c:P * c + P] for c in range(4)], NT), "qgT")
                after(pe, DVE, k, "qgT")
                for h in range(H):
                    half = slice(64 * (h % 2), 64 * (h % 2) + 64)
                    last = pe.matmul(pq[:, h % 2, NT * (h // 2):NT * (h // 2) + NT], w_ukT[half, h // 2, :],
                                     rt_s[half, NT * (h // 2):NT * (h // 2) + NT], start=True, stop=True)
                signal(last, "qabs")
                after(pe, DVE, k, "qr")
                signal(transposes(pp[:, 0], [sq_s[0:NT, 512 + P * h:512 + P * h + P] for h in range(H)], NT), "qrT")
                after(pe, DVE, k, "pages_f")
                signal(pe.matmul(pp[:, 1, 0:16], const("sel16", NT), ptab_f[:, :], start=True, stop=True), "pages")

            def cache(k, b):
                begin(pe, k)
                pe.wait_ge(kv_in, 32 * (b + 1))
                kn_bank = (pp, pq)

                def tiles_T(g):
                    signal(transposes(ps[1], [kv[:, 4 * g + i, :] for i in range(4)], P), f"cT{g}")

                def keys_of(j):
                    if j >= 2:
                        after(pe, ACTE, k, f"sq{j - 2}")
                    for i in range(2):
                        tile = 2 * j + i
                        lhs = cTc[:, P * (tile % 8):P * (tile % 8) + P]
                        pe.matmul(kn_bank[j % 2][:, i], lhs, w_uk[:, :], start=True, stop=True)
                        last = pe.matmul(ps[0][:, H * tile:H * tile + H], lhs, qabs[:, b, :], start=False,
                                         stop=True, skip_group_check=True)
                    signal(last, f"kn{j}")

                point(k, 0)
                if not rope_before(b):
                    after(pe, DVE, k, "rope")
                signal(transposes(ps[1], [krr[:, P * g:P * g + P] for g in range(4)], P), "krT")
                after(pe, ACTE, k, "krT")
                for g in range(4):
                    pe.matmul(ps[0][:, 32 * g:32 * g + 32], krT[:, P * g:P * g + P],
                              qpad[:, b].rearrange("p i h -> p (i h)"), start=g == 0, stop=False, skip_group_check=True)
                tiles_T(0)
                for g in range(4):
                    after(pe, ACTE, k, f"cT{g}")
                    if g == 0:
                        tiles_T(1)
                        keys_of(0)
                        keys_of(1)
                    else:
                        if g < 3:
                            tiles_T(g + 1)
                        keys_of(2 * g)
                        keys_of(2 * g + 1)
                    point(k, 1 + g)
                after(pe, DVE, k, "max")
                signal(pe.transpose(ps[1][0:H, 0:P], scr[:, 32:40], ident), "maxT")
                after(pe, DVE, k, "diag")
                signal(pe.matmul(ps[1][:, 128:136], ones[0:H, :], scr[0:H, 48:56], start=True, stop=True), "maxb")
                after(pe, DVE, k, "sum")
                pe.matmul(ps[1][:, 256:264], ones, scr[:, 40:48], start=True, stop=True)
                for i in range(16):
                    pe.matmul(ps[1][:, 264:272], kv[:, i, :], pr[:, H * i:H * i + H], start=i == 0, stop=False)
                signal(pe.matmul(ps[1][:, 264:272], ckv[S][0:NT, :], pr[0:NT, 16 * H:17 * H], start=False, stop=True), "pv")
                point(k, 5)

            def cache_out(k):
                begin(pe, k)
                for h in range(H):
                    last = pe.matmul(ps[0][:, NT * h:NT * h + NT], w_uv[:, VD * h:VD * h + VD], olS[:, h, :],
                                     start=True, stop=True)
                signal(last, "oT")

            def sgu_init(k):
                begin(pe, k)
                pe.wait_ge(sgu_in, 64)
                for q in range(3):
                    signal(transposes((ps[0], ps[1], pq[:, 0])[q], [sv[:, P * g:P * g + P] for g in range(4 * q, 4 * q + 4)], P),
                           f"wT{q}")

            def sgu_v(k, tile, j):
                begin(pe, k)
                w, out = chunk(k, 0, 8), ps[j % 2][:, 0:256]
                for c in range(KD):
                    pe.matmul(out, hT[:, c, :], w[:, c, :], start=c == 0, stop=False)
                signal(pe.matmul(out, ones[0:1, :], rows[0:1, 256 * j:256 * j + 256], start=False, stop=True), "v")

            def sgu_u(k, tile, j):
                begin(pe, k)
                w = chunk(k, 0, 8)
                for side in range(2):
                    out, at = ps[j % 2][:, P * side:P * side + P], 256 * j + P * side
                    for c in range(KD):
                        pe.matmul(out, w[:, c, P * side:P * side + P], hT[:, c, :], start=c == 0, stop=False)
                    last = pe.matmul(out, rows[32:33, at:at + P], ones[32:33, :], start=False, stop=True)
                signal(last, "u")

            def sgu_mix(k, tile):
                begin(pe, k)
                if tile == B:
                    pe.wait_ge(v_out, 16)
                for q in range(3):
                    out = (ps[0], ps[1], pq[:, 0])[q]
                    for i in range(4):
                        g, acc = 4 * q + i, out[:, P * i:P * i + P]
                        pe.matmul(acc, ones[64:65, :], rows[64:65, P * g:P * g + P], start=True, stop=False)
                        last = pe.matmul(acc, sv[:, P * g:P * g + P], wcT[:, P * g:P * g + P], start=False, stop=True)
                signal(last, "s")
                point(k, 0)

            def sgu_s(k, j):
                begin(pe, k)
                w, out = chunk(k, 0, 8), ps[j % 2][0:NT, 0:256]
                part_, at = (32, 256 * j) if j < 6 else (0, 256 * j - SGH)
                for c in range(KD):
                    pe.matmul(out, hT[:, c, 0:NT], w[:, c, :], start=c == 0, stop=False)
                signal(pe.matmul(out, ones[part_:part_ + 1, 0:NT], rows[part_:part_ + 1, at:at + 256],
                                 start=False, stop=True), "z")

            def sgu_s_mix(k):
                point(k, 0)
                point(k, 1)
                begin(pe, k)
                pe.wait_ge(v_out, 32)
                after(pe, DVE, k, "gated")
                signal(transposes(ps[0], [stmp[0:NT, P * g:P * g + P] for g in range(SGG)], NT), "gT")

            def unit(g):
                slot = g - LAG
                if slot < 0:
                    return
                p = STEP_OF[slot]
                n, h = STEPS[p]
                first = slot == SLOT0[p] and h in (None, 0)
                final = slot == SLOT0[p + 1] - 1 and h in (None, PH - 1)
                if h is None and first:
                    k = WHERE[("peer_out", n)]
                    for e in (PE, DVE, ACTE):
                        pe.wait_ge(stage_done[e], BASE[k][e])
                elif first and p:
                    after(pe, DVE, WHERE[("peer_out", {1: 0, 3: 1, 4: 3}[n])], "x")
                elif first:
                    pe.wait_ge(mod_done[DVE], MODS0[WHERE[("query", 0, 0)]])
                out, r = (pp, NT) if h is None else (yacc, P)
                pe.wait_ge(v_land[slot % RING], 16 * (slot // RING + 1))
                pe.wait_ge(diag_ready, slot + 1)
                for q in range(2):
                    last = pe.matmul(out[0:r, q], diag[:, slot % RING, 0:r], vring[:, slot % RING, 512 * q:512 * q + 512],
                                     start=first, stop=final)
                last.then_inc(v_used, 1)

            def point(k, j):
                early_or_units(k, j, PE, mod, unit, lambda g: None)

            stages = dict(init=init, tables=tables, mod=mod, norm=norm, mla_in=mla_in, attn=attn, proj=proj, query=query,
                          query_s=query_s, cache_init=cache_init, cache=cache, cache_out=cache_out,
                          sgu_init=sgu_init, sgu_v=sgu_v, sgu_u=sgu_u, sgu_mix=sgu_mix, sgu_s=sgu_s,
                          sgu_s_mix=sgu_s_mix, sgu_out=sgu_out)
            for k, s in enumerate(SCHEDULE):
                signal.start(k)
                if s[0] in stages:
                    stages[s[0]](k, *s[1:])
                else:
                    for j in range(n_points(k) - 1):
                        point(k, j)
                point(k, n_points(k) - 1)
                signal.end()

        @block.scalar
        def _(act):
            signal = Signals(act, ACTE)
            chain = [0]

            def link(ins):
                chain[0] += 1
                ins.then_inc(act_chain, 1)
                act.wait_ge(act_chain, chain[0])

            def copy(out, in_):
                return act.activation(out, in_, ACT.Copy)

            def init(k):
                act.wait_ge(in_first, 48)
                signal(act.activation(h_tok[A][0:9, :], h_rep[0:9, :], ACT.Tanh, scale=0.5), "tanh")

            def norm(k, tile, layer, second):
                point(k, 0)
                begin(act, k)
                r = ROWS[tile]
                for q in range(2):
                    after(act, PE, k, f"hT{q}")
                    signal(copy(hT[:, 4 * q:4 * q + 4, 0:r], ps[q][:, 0:4 * r].rearrange("p (c t) -> p c t", c=4)), f"hT{q}")
                if tile == S and second:
                    after(act, PE, k, "rep")
                    signal(copy(h_rep[:, :], pp[:, :, :].rearrange("p q n -> p (q n)")), "rep")

            def mla_in(k, tile):
                begin(act, k)
                r = ROWS[tile]
                z, cT, qk, sq = (shape_of(tile, a, b) for a, b in ((z_, z_s), (cT_, cT_s), (qk_, qk_s), (sq_, sq_s)))
                after(act, PE, k, "z")
                signal(copy(z[0:r, :], ps[0][0:r, 0:416]), "z")
                point(k, 0)
                after(act, PE, k, "cT")
                signal(copy(cT[:, 0:3 * r], ps[1][:, 0:3 * r]), "cT")
                after(act, PE, k, "qk")
                copy(qk[0:r, 0:480], pp[0:r, 0, 0:480])
                copy(qk[0:r, 480:768], pp[0:r, 1, 0:288])
                keys = qk[0:r, 768:1536].rearrange("p (h d) -> p h d", h=H)
                signal(copy(keys[:, :, 0:NOPE], ps[0][0:r, :].rearrange("p (h d) -> p h d", h=H)), "qk")
                after(act, ACTE, k, "qk")
                after(act, DVE, k, "kr")
                signal(act.activation(sq[0:r, :], qk[0:r, :], ACT.Square), "sq")
                point(k, 1)

            def attn(k, tile):
                begin(act, k)
                kt = 1 + tile
                for f in range(2):
                    after(act, PE, k, f"kT{f}")
                    signal(copy(kT[tile][0:QK, 512 * f:512 * f + 512], pq[0:QK, f]), f"kT{f}")
                for f in range(2):
                    after(act, DVE, k, f"max{f}")
                    n = P * kt
                    for i in range(4):
                        last = act.activation(prob[:, n * i:n * i + n], att[:, n * i:n * i + n], ACT.Exp,
                                              bias=scr[:, 4 + i:5 + i], scale=SM_SCALE, accum_out=scr[:, 8 + i:9 + i])
                    signal(last, f"exp{f}")
                    point(k, f)
                    for q in range(kt):
                        after(act, PE, k, f"pT{f}{q}")
                        signal(copy(att[:, 512 * q:512 * q + 512], ps[q][:, :]), f"pT{f}{q}")

            def query(k, n, h):
                begin(act, k)
                after(act, PE, k, "q")
                signal(copy(qs[:, :, :], ps[0][:, 0:256].rearrange("p (i t) -> p i t", i=2)), "q")
                point(k, 0)
                after(act, PE, k, "s")
                signal(copy(sc[:, :, :], ps[1][:, 0:256].rearrange("p (i t) -> p i t", i=2)), "s")
                point(k, 1)
                pick_exp(k, P)

            def pick_exp(k, r):
                after(act, DVE, k, "top")
                signal(act.activation(eg[0:r, 0:TOPK], ctop[0:r, :], ACT.Exp, bias=eg[0:r, TOPK:TOPK + 1],
                                      accum_out=eg[0:r, TOPK + 1:TOPK + 2]), "exp")

            def query_s(k, n):
                begin(act, k)
                for h in range(PH):
                    after(act, PE, k, f"q{h}")
                    signal(copy(q_s[0:NT, 256 * h:256 * h + 256], ps[h % 2][0:NT, 0:256]), f"q{h}")
                    point(k, h)
                after(act, PE, k, "qT")
                for side in range(2):
                    last = copy(qs[:, side, 0:64].rearrange("p (b h) -> p h b", h=PH),
                                ps[0][:, 64 * side:64 * side + 64].rearrange("p (h b) -> p h b", h=PH))
                signal(last, "qT")
                after(act, PE, k, "s")
                signal(copy(sc[0:64, :, :], ps[1][0:64, 0:256].rearrange("p (i t) -> p i t", i=2)), "s")

            def topk_s(k, n):
                begin(act, k)
                point(k, 0)
                pick_exp(k, 64)

            def cache(k, b):
                begin(act, k)
                kn_bank = (pp, pq)
                point(k, 0)


                def key_squares(b, plus):
                    after(act, DVE, k, "rope" + plus)
                    signal(act.activation(krsq, kr[:, b % 2].rearrange("p r j -> p (r j)"), ACT.Square), "krsq" + plus)

                if not rope_before(b):
                    key_squares(b, "")
                after(act, PE, k, "krT")
                signal(copy(krT, ps[1][:, :]), "krT")

                def latents(g):
                    after(act, PE, k, f"cT{g}")
                    if g >= 2:
                        after(act, PE, k, f"kn{2 * g - 3}")
                    signal(copy(cTc[:, 512 * (g % 2):512 * (g % 2) + 512], ps[1][:, :]), f"cT{g}")

                def squares(j):
                    after(act, PE, k, f"kn{j}")
                    if j < 2 and not rope_before(b):
                        after(act, DVE, k, "krsq")
                    if j >= 2:
                        after(act, DVE, k, f"ssn{j - 2}")
                    signal(act.activation(knsq[:, 1024 * (j % 2):1024 * (j % 2) + 1024],
                                          kn_bank[j % 2][:, :, :].rearrange("p i n -> p (i n)"), ACT.Square), f"sq{j}")

                latents(0)
                for g in range(4):
                    if g < 3:
                        latents(g + 1)
                    squares(2 * g)
                    squares(2 * g + 1)
                    point(k, 1 + g)
                after(act, DVE, k, "shift")
                signal(act.activation(pr, pr, ACT.Exp, scale=SM_SCALE), "exp")
                if b + 1 < NT and rope_before(b + 1):
                    key_squares(b + 1, "+")
                point(k, 5)

            def sgu_v(k, tile, j):
                begin(act, k)
                after(act, PE, k, "v")
                signal(copy(sv[:, 256 * j:256 * j + 256], ps[j % 2][:, 0:256]), "v")

            def sgu_vnorm(k, tile):
                begin(act, k)
                after(act, DVE, k, "poly")
                signal(act.activation(stmp, stmp, ACT.Tanh, scale=GELU_K), "tanh")
                point(k, 0)

            def sgu_u(k, tile, j):
                begin(act, k)
                after(act, PE, k, "u")
                signal(copy(su[:, 256 * j:256 * j + 256], ps[j % 2][:, 0:256]), "u")

            def sgu_s(k, j):
                begin(act, k)
                after(act, PE, k, "z")
                dst = su[0:NT, 256 * j:256 * j + 256] if j < 6 else sv[0:NT, 256 * j - SGH:256 * j - SGH + 256]
                signal(copy(dst, ps[j % 2][0:NT, 0:256]), "z")

            def sgu_s_mix(k):
                begin(act, k)
                after(act, DVE, k, "poly")
                act.activation(stmp[0:NT, :], stmp[0:NT, :], ACT.Tanh, scale=GELU_K)
                signal(act.activation(rows[0:NT, :], rows[0:NT, :], ACT.Tanh, scale=GELU_K), "tanh")
                point(k, 0)
                point(k, 1)

            def diagonal(g):
                slot = g - LAG + DIAG_AHEAD
                if 0 <= slot < N_SLOTS:
                    p = STEP_OF[slot]
                    h = STEPS[p][1]
                    if slot == SLOT0[p]:
                        act.wait_ge(w_ready, p + 1)
                    if slot >= RING:
                        act.wait_ge(v_used, slot - RING + 1)
                    base = const("selt") if h is None else ident
                    act.activation(diag[:, slot % RING, 0:base.shape[-1]], base, ACT.Copy,
                                   scale=wts[:, p % 2, slot - SLOT0[p]:slot - SLOT0[p] + 1]).then_inc(diag_ready, 1)

            def tanh(g):
                if g < N_SLOTS and g == SLOT0[STEP_OF[g] + 1] - 1:
                    p = STEP_OF[g]
                    act.wait_ge(poly_ready, p + 1)
                    act.activation(ew[:, 2, 0:SLOTS[p]], ew[:, 0, 0:SLOTS[p]], ACT.Tanh, scale=GELU_K)\
                       .then_inc(tanh_ready, 1)

            def point(k, j):
                early_or_units(k, j, ACTE, lambda *a: None, diagonal, tanh)

            stages = dict(init=init, norm=norm, mla_in=mla_in, attn=attn, query=query, query_s=query_s, topk_s=topk_s,
                          cache=cache, sgu_v=sgu_v, sgu_vnorm=sgu_vnorm, sgu_u=sgu_u, sgu_mix=sgu_vnorm,
                          sgu_s=sgu_s, sgu_s_mix=sgu_s_mix)
            for k, s in enumerate(SCHEDULE):
                signal.start(k)
                if s[0] in stages:
                    stages[s[0]](k, *s[1:])
                else:
                    for j in range(n_points(k) - 1):
                        point(k, j)
                point(k, n_points(k) - 1)
                signal.end()

        @block.vector
        def _(dve):
            signals = Signals(dve, DVE)
            chain = [0]

            def link(ins):
                chain[0] += 1
                ins.then_inc(dve_chain, 1)
                dve.wait_ge(dve_chain, chain[0])

            def signal(ins, name):
                signals(ins, name)
                after(dve, DVE, signals.k, name)

            tt, ts, stt, cp = dve.tensor_tensor, dve.tensor_scalar, dve.scalar_tensor_tensor, dve.tensor_copy

            def over(a, n):
                return a.unsqueeze(2).to_broadcast([a.shape[0], a.shape[1], n])

            def times(a, n):
                return a.unsqueeze(1).to_broadcast([a.shape[0], n, a.shape[1]])

            def rsqrt(out, v, tmp):
                link(ts(out.bitcast(U32), v.bitcast(U32), 1, None, ALU.logical_shift_right))
                link(ts(out.bitcast(U32), out.bitcast(U32), -1.0, RSQRT_MAGIC, ALU.mult, ALU.add))
                for _ in range(3):
                    link(tt(tmp, out, out, ALU.mult))
                    link(tt(tmp, tmp, v, ALU.mult))
                    link(ts(tmp, tmp, -0.5, 1.5, ALU.mult, ALU.add))
                    link(tt(out, out, tmp, ALU.mult))

            def square_sum(out, a, waste):
                link(dve.tensor_tensor_reduce(waste, a, a, 1.0, 0.0, ALU.mult, ALU.add, out))

            def init(k):
                dve.wait_ge(in_first, 48)
                after(dve, ACTE, k, "tanh")
                c, th = h_rep[0:9, :], h_tok[A][0:9, :]
                link(stt(c, th, 1.0, c, ALU.add, ALU.mult))
                signal(ts(c, c, 0.5, None, ALU.mult), "silu")
                after(dve, PE, k, "cT")
                signal(cp(siluT[:, :, :], ps[0][:, 0:16 * KD].rearrange("p (c t) -> p c t", c=KD)[:, :, 0:9]), "siluT")

            def tables(k):
                begin(dve, k)
                dve.wait_ge(in_once, 16 * N_ONCE)
                after(dve, PE, k, "keysT")
                signal(cp(keysT[:, :, :].rearrange("p i n -> p (i n)"), ps[1][:, :]), "keysT")
                after(dve, PE, k, "ukT")
                signal(cp(w_ukT[:, :, :].rearrange("p i n -> p (i n)"), pp[:, 0]), "ukT")

            def mod(k, l, j):
                i = MODS.index(("mod", l, j))
                dve.wait_ge(mod_done[PE], i + 1)
                dve.wait_ge(mbias_in[i % 2], 32 * (i // 2 + 1))
                if i >= 2:
                    dve.wait_ge(mrow_out[i % 2], 16 * (i // 2))
                out, acc = mrow[:, i % 2, :], mod_bank(i)[0:9, 0:256]
                if j // 4 in (1, 4):
                    link(tt(out, acc, mbg[:, i % 2, 0, :], ALU.add))
                    ins = stt(out, out, 1.0, mbg[:, i % 2, 1, :], ALU.add, ALU.mult)
                else:
                    ins = tt(out, acc, mbg[:, i % 2, 0, :], ALU.add)
                ins.then_inc(mod_done[DVE], 1)

            def norm(k, tile, layer, second):
                begin(dve, k)
                r, n = ROWS[tile], NORMS.index(k)
                xr, h = x[tile][0:r, :], h_tok[tile][0:r, :]
                if n == 0:
                    dve.wait_ge(in_x, 16)
                square_sum(scr[0:r, 0:1], xr, h)
                link(ts(scr[0:r, 0:1], scr[0:r, 0:1], 1.0 / D, EPS, ALU.mult, ALU.add))
                rsqrt(scr[0:r, 1:2], scr[0:r, 0:1], rs[0:r, 0:1])
                dve.wait_ge(g_land, 16 * (GAINS.index(k) + 1))
                link(stt(h, xr, scr[0:r, 1:2], modg[0:r, :], ALU.mult, ALU.mult))
                dve.wait_ge(s_land, 16 * (n + 1))
                signal(tt(h, h, mods[0:r, :], ALU.add), "h")
                point(k, 0)

            def rotate(a, cos, sin, tmp, out=None):
                n = a.shape[1]
                x1, x2 = a[:, :, 0:HALF], a[:, :, HALF:ROPE]
                m = [tmp[:, HALF * n * i:HALF * n * (i + 1)].rearrange("p (n j) -> p n j", n=n) for i in range(4)]
                link(tt(m[0], x1, cos, ALU.mult))
                link(tt(m[1], x2, sin, ALU.mult))
                link(tt(m[2], x2, cos, ALU.mult))
                link(tt(m[3], x1, sin, ALU.mult))
                link(tt(x1, m[0], m[1], ALU.subtract))
                return tt(x2, m[2], m[3], ALU.add)

            def mla_in(k, tile):
                begin(dve, k)
                r = ROWS[tile]
                z, qk, sq, rt = (shape_of(tile, a, b)[0:r, :] for a, b in ((z_, z_s), (qk_, qk_s), (sq_, sq_s), (rt_, rt_s)))
                after(dve, ACTE, k, "z")
                if tile == A:
                    dve.wait_ge(in_once, 16 * N_ONCE)
                square_sum(scr[0:r, 0:1], z[:, 0:QR], sq[:, 0:QR])
                square_sum(scr[0:r, 1:2], z[:, QR:QR + KVR], sq[:, 0:KVR])
                link(ts(scr[0:r, 0:1], scr[0:r, 0:1], 1.0 / QR, EPS, ALU.mult, ALU.add))
                link(ts(scr[0:r, 1:2], scr[0:r, 1:2], 1.0 / KVR, EPS, ALU.mult, ALU.add))
                rsqrt(scr[0:r, 2:4], scr[0:r, 0:2], rs[0:r, 0:2])
                link(cp(krt[tile][0:r, :], z[:, QR + KVR:416]))
                link(stt(z[:, 0:QR], z[:, 0:QR], scr[0:r, 2:3], gqa[0:r, :], ALU.mult, ALU.mult))
                signal(stt(ckv[tile][0:r, :], z[:, QR:QR + KVR], scr[0:r, 3:4], gkva[0:r, :], ALU.mult, ALU.mult), "c")
                q4 = qk.rearrange("p (i h d) -> p i h d", i=2, h=H)
                q3 = qk.rearrange("p (i d) -> p i d", i=2 * H)
                signal(cp(q4[:, 1, :, NOPE:QK], times(krt[tile][0:r, :], H)), "kr")
                point(k, 0)
                point(k, 1)
                after(dve, ACTE, k, "sq")
                s16, v16 = scr[0:r, 16:32], scr[0:r, 32:48]
                link(dve.tensor_reduce(v16, sq.rearrange("p (i d) -> p i d", i=2 * H), X, ALU.add))
                link(ts(v16, v16, 1.0 / QK, EPS, ALU.mult, ALU.add))
                rsqrt(s16, v16, rs[0:r, 0:16])
                link(tt(q3, q3, over(s16, QK), ALU.mult))
                for i in range(2):
                    link(tt(q4[:, i], q4[:, i], times(gqk[0:r, QK * i:QK * i + QK], H), ALU.mult))
                if tile == S:
                    cos, sin = const("cos_q", r), const("sin_q", r)
                else:
                    cos, sin = (const(c)[:, HALF * tile:HALF * tile + HALF] for c in ("cos_p", "sin_p"))
                signal(rotate(q3[:, :, NOPE:QK], times(cos, 2 * H), times(sin, 2 * H), rt), "qk")

            def attn(k, tile):
                begin(dve, k)
                kt = 1 + tile
                for f in range(2):
                    after(dve, PE, k, f"qT{f}")
                    signal(cp(qT[0:QK, 512 * f:512 * f + 512], ps[f][0:QK, :]), f"qT{f}")
                for f in range(2):
                    after(dve, PE, k, f"s{f}")
                    s4 = pp[:, :, :].rearrange("p q n -> p (q n)")[:, 0:512 * kt].rearrange("p (h q k) -> p h q k", h=4, q=kt)
                    a4 = att[:, 0:512 * kt].rearrange("p (h q k) -> p h q k", h=4, q=kt)
                    if f:
                        after(dve, PE, k, "ol0")
                    if kt == 2:
                        link(cp(a4[:, :, 0], s4[:, :, 0]))
                    link(tt(a4[:, :, kt - 1], s4[:, :, kt - 1], times(const("cmask"), 4), ALU.add))
                    link(dve.tensor_reduce(scr[:, 0:4], att[:, 0:512 * kt].rearrange("p (h n) -> p h n", h=4), X, ALU.max))
                    signal(ts(scr[:, 4:8], scr[:, 0:4], -SM_SCALE, None, ALU.mult), f"max{f}")
                    point(k, f)
                    after(dve, ACTE, k, f"exp{f}")
                    link(dve.reciprocal(scr[:, 12:16], scr[:, 8:12]))
                    p3 = prob[:, 0:512 * kt].rearrange("p (h n) -> p h n", h=4)
                    signal(tt(p3, p3, over(scr[:, 12:16], P * kt), ALU.mult), f"p{f}")
                    after(dve, PE, k, f"ol{f}")
                    signal(cp(ol[:, 512 * f:512 * f + 512], pq[:, f]), f"ol{f}")
                after(dve, PE, k, "oT")
                link(cp(oT[:, 0:512], ps[0][:, :]))
                signal(cp(oT[:, 512:1024], ps[1][:, :]), "oT")

            def residual(k, tile, acc):
                r = ROWS[tile]
                dve.wait_ge(g_land, 16 * (GAINS.index(k) + 1))
                h = h_tok[tile][0:r, :]
                link(tt(h, acc[0:r, :, :].rearrange("p q n -> p (q n)"), modg[0:r, :], ALU.mult))
                signal(tt(x[tile][0:r, :], x[tile][0:r, :], h, ALU.add), "x")

            def proj(k, tile):
                begin(dve, k)
                for i in range(4):
                    point(k, i)
                after(dve, PE, k, "w3")
                residual(k, tile, pp)

            def sgu_out(k, tile):
                begin(dve, k)
                for i in range(6):
                    point(k, i)
                after(dve, PE, k, "w5")
                residual(k, tile, pp)

            def peer_out(k, n):
                begin(dve, k)
                last = max(p for p, s in enumerate(STEPS) if s[0] == n)
                dve.wait_ge(v_used, SLOT0[last + 1])
                residual(k, n % 3, pp if n % 3 == S else yacc)

            def top16(vals, index, a, scratch, r):
                link(dve.max(vals[:, 0:8], a))
                link(dve.match_replace(scratch, vals[:, 0:8], a, -3e38))
                link(dve.max_index(index[:, 0:8], vals[:, 0:8], a))
                link(dve.max(vals[:, 8:16], scratch))
                link(dve.max_index(index[:, 8:16], vals[:, 8:16], scratch))

            def route(k, mid, r, expert_out, gate_out):
                for i in range(2):
                    top16(t1[0:r, i, :], ti[0:r, i, :], sc[0:r, i, :], work[0:r, 0:NKEYS], r)
                c3 = cand[0:r, :].rearrange("p (a b) -> p a b", a=TOPK)
                link(tt(c3, over(t1[0:r, 0, :], TOPK), times(t1[0:r, 1, :], TOPK), ALU.add))
                top16(ctop[0:r, :], ci[0:r, :], cand[0:r, :], work[0:r, :], r)
                signal(ts(eg[0:r, TOPK:TOPK + 1], ctop[0:r, 0:1], -1.0, None, ALU.mult), "top")
                point(k, mid)
                link(ts(cu[0:r, 0, :], ci[0:r, :], 4, None, ALU.logical_shift_right))
                link(ts(cu[0:r, 1, :], ci[0:r, :], 15, None, ALU.bitwise_and))
                link(cp(cf[0:r, 0:2, :], cu[0:r, :, :]))
                link(cp(cf[0:r, 2:4, :], ti[0:r, :, :]))
                for i in range(2):
                    hr = hot[0:r, :, :]
                    link(tt(hr, over(cf[0:r, i, :], TOPK), times(const("iota16", r), TOPK), ALU.is_equal))
                    link(tt(hr, hr, times(cf[0:r, 2 + i, :], TOPK), ALU.mult))
                    link(dve.tensor_reduce(ef[0:r, i, :], hr, X, ALU.add))
                link(stt(expert_out, ef[0:r, 0, :], float(NKEYS), ef[0:r, 1, :], ALU.mult, ALU.add))
                after(dve, ACTE, k, "exp")
                link(dve.reciprocal(eg[0:r, TOPK + 2:TOPK + 3], eg[0:r, TOPK + 1:TOPK + 2]))
                signal(ts(gate_out, eg[0:r, 0:TOPK], eg[0:r, TOPK + 2:TOPK + 3], 0.5, ALU.mult, ALU.mult), "topk")

            def query(k, n, h):
                point(k, 0)
                begin(dve, k)
                after(dve, ACTE, k, "s")
                route(k, 1, P, expert[n % 3][:, h, :], gate[n % 3][:, h, :])

            def topk_s(k, n):
                begin(dve, k)
                route(k, 0, 64, topi_s[:, :], top_s[:, :])

            def cache_init(k):
                begin(dve, k)
                q4 = qk_s[0:NT, :].rearrange("p (i h d) -> p i h d", i=2, h=H)
                q, key = q4[:, 0], q4[:, 1]
                gn = times(gqk[0:NT, QK:QK + NOPE], H)
                signal(tt(sq_s[0:NT, 0:512].rearrange("p (h d) -> p h d", h=H), q[:, :, 0:NOPE], gn, ALU.mult), "qg")
                rep = sq_s[0:NT, 512:1536].rearrange("p (h i j) -> p h i j", h=H, i=4)
                for i in range(3):
                    link(cp(rep[:, :, i], q[:, :, NOPE:QK]))
                signal(cp(rep[:, :, 3], q[:, :, NOPE:QK]), "qr")
                dve.wait_ge(pages_in, 32)
                signal(cp(ptab_f[:, :], ptab[:, :]), "pages_f")
                point(k, 0)
                m = rt_s[0:NT, 0:H * QK].rearrange("p (h d) -> p h d", h=H)
                link(tt(m, q, key, ALU.mult))
                link(dve.tensor_reduce(own[:, :], m, X, ALU.add))
                link(dve.memset(scores[:, :, :], NEG))
                link(dve.memset(qpad[:, :, :, :], 0.0))
                after(dve, PE, k, "qgT")
                signal(cp(rt_s[:, 0:32], ps[0][:, 0:32]), "qgT")
                after(dve, PE, k, "qabs")
                for i in range(2):
                    ins = cp(qabs[:, :, :].rearrange("p b (h i) -> p i h b", i=2)[:, i],
                             pq[:, i, 0:32].rearrange("p (h b) -> p h b", h=4))
                    if i == 0:
                        link(ins)
                signal(ins, "qabs")
                after(dve, PE, k, "qrT")
                for i in range(4):
                    at = slice(32 * i, 32 * i + 32)
                    ins = cp(qpad[at, :, i, :].rearrange("p b h -> p h b"),
                             pp[at, 0, 0:64].rearrange("p (h b) -> p h b", h=H))
                    if i < 3:
                        link(ins)
                signal(ins, "qpad")
                after(dve, PE, k, "pages")
                signal(ts(page_rows[:, :], pp[:, 1, 0:16], 16.0, const("pmod"), ALU.mult, ALU.add), "pages")

            def cache(k, b):
                begin(dve, k)
                def rope(b, plus):
                    dve.wait_ge(kr_in[b % 2], 32 * (b // 2 + 1))
                    r3 = krr.rearrange("p (t j) -> p t j", t=16)
                    link(tt(r3, kr[:, b % 2], times(gqk[:, QK + NOPE:2 * QK], 16), ALU.mult))
                    cos, sin = (const(c).rearrange("p (t j) -> p t j", t=16) for c in ("cos_c", "sin_c"))
                    signal(rotate(r3, cos, sin, rope_t), "rope" + plus)

                def key_square_sums(plus):
                    after(dve, ACTE, k, "krsq" + plus)
                    signal(dve.tensor_reduce(scr[:, 16:32], krsq.rearrange("p (t j) -> p t j", t=16), X, ALU.add),
                           "krsq" + plus)

                if not rope_before(b):
                    rope(b, "")
                point(k, 0)
                if not rope_before(b):
                    key_square_sums("")
                for j in range(8):
                    after(dve, ACTE, k, f"sq{j}")
                    signal(dve.tensor_reduce(ssn[:, 16 * j:16 * j + 16],
                                             knsq[:, 1024 * (j % 2):1024 * (j % 2) + 1024].rearrange("p (i d) -> p i d", d=NOPE),
                                             X, ALU.add), f"ssn{j}")
                    if j % 2 and j < 7:
                        point(k, 1 + j // 2)
                n3 = ssn.rearrange("p (t h) -> p t h", t=16)
                link(tt(n3, n3, over(scr[:, 16:32], H), ALU.add))
                link(ts(ssn, ssn, 1.0 / QK, EPS, ALU.mult, ALU.add))
                rsqrt(rkk, ssn, pr[:, 0:128])
                after(dve, PE, k, "kn7")
                link(tt(scores[:, 0:16, :].rearrange("p t h -> p (t h)"), ps[0][:, 0:128], rkk, ALU.mult))
                link(ts(scores[0:NT, 16, :], own[:, :], const("own_neg", NT)[:, b:b + 1], None, ALU.add))
                signal(dve.tensor_reduce(scr[:, 32:40], scores[:, :, :].rearrange("p t h -> p h t"), X, ALU.max), "max")
                point(k, 4)
                after(dve, PE, k, "maxT")
                link(dve.tensor_reduce(scr[0:H, 56:57], ps[1][0:H, 0:P], X, ALU.max))
                signal(ts(scr[0:H, 48:56], ident[0:H, 0:H], scr[0:H, 56:57], None, ALU.mult), "diag")
                after(dve, PE, k, "maxb")
                link(cp(scr[:, 0:8], ps[1][:, 128:136]))
                p3 = pr.rearrange("p (t h) -> p t h", t=17)
                signal(tt(p3, scores[:, :, :], times(scr[:, 0:8], 17), ALU.subtract), "shift")
                after(dve, ACTE, k, "exp")
                signal(dve.tensor_reduce(scr[:, 40:48], pr.rearrange("p (t h) -> p h t", t=17), X, ALU.add), "sum")
                ahead = b + 1 < NT and rope_before(b + 1)
                if ahead:
                    rope(b + 1, "+")
                point(k, 5)
                after(dve, PE, k, "pv")
                link(dve.reciprocal(scr[:, 8:16], ps[1][:, 256:264]))
                signal(tt(olS[:, :, b], ps[1][:, 264:272], scr[:, 8:16], ALU.mult), "ol")
                if ahead:
                    key_square_sums("+")

            def cache_out(k):
                begin(dve, k)
                after(dve, PE, k, "oT")
                signal(cp(oTs, ps[0][:, 0:64]), "oT")

            def sgu_init(k):
                begin(dve, k)
                for q in range(3):
                    after(dve, PE, k, f"wT{q}")
                    out = (ps[0], ps[1], pq[:, 0])[q]
                    signal(tt(wcT[:, 512 * q:512 * q + 512].rearrange("p (g t) -> p g t", g=4),
                              out[:, :].rearrange("p (g t) -> p g t", g=4), times(const("cmask_t"), 4), ALU.mult), f"wT{q}")

            def polynomial(out, a):
                link(tt(out, a, a, ALU.mult))
                link(ts(out, out, GELU_C, 1.0, ALU.mult, ALU.add))
                return tt(out, out, a, ALU.mult)

            def norm_v(r, waste, g, name):
                v = sv[0:r, :]
                square_sum(scr[0:r, 0:1], v, waste)
                link(ts(scr[0:r, 0:1], scr[0:r, 0:1], 0.25 / SGH, EPS, ALU.mult, ALU.add))
                rsqrt(scr[0:r, 1:2], scr[0:r, 0:1], rs[0:r, 0:1])
                link(ts(scr[0:r, 2:3], scr[0:r, 1:2], 0.5, None, ALU.mult))
                signal(stt(v, v, scr[0:r, 2:3], g, ALU.mult, ALU.mult), name)

            def sgu_vnorm(k, tile):
                begin(dve, k)
                signal(polynomial(stmp, sv), "poly")
                point(k, 0)
                after(dve, ACTE, k, "tanh")
                link(stt(sv, stmp, 1.0, sv, ALU.add, ALU.mult))
                dve.wait_ge(gv_in, 16 * (tile + 1))
                norm_v(P, stmp, su, "v")

            def sgu_mix(k, tile):
                begin(dve, k)
                signal(polynomial(stmp, su), "poly")
                point(k, 0)
                after(dve, ACTE, k, "tanh")
                link(stt(su, stmp, 1.0, su, ALU.add, ALU.mult))
                after(dve, PE, k, "s")
                for q in range(3):
                    at = slice(512 * q, 512 * q + 512)
                    ins = stt(su[:, at], (ps[0], ps[1], pq[:, 0])[q][:, :], 0.5, su[:, at], ALU.mult, ALU.mult)
                    if q < 2:
                        link(ins)
                signal(ins, "gated")

            def sgu_s_mix(k):
                begin(dve, k)
                r = slice(0, NT)
                link(polynomial(stmp[r, :], su[r, :]))
                signal(polynomial(rows[r, :], sv[r, :]), "poly")
                point(k, 0)
                after(dve, ACTE, k, "tanh")
                link(stt(su[r, :], stmp[r, :], 1.0, su[r, :], ALU.add, ALU.mult))
                link(stt(sv[r, :], rows[r, :], 1.0, sv[r, :], ALU.add, ALU.mult))
                dve.wait_ge(gv_in, 48)
                norm_v(NT, stmp[r, :], wcT[r, :], "v")
                point(k, 1)
                dve.wait_ge(w00_in, 32)
                s3, v3 = (a[r, :].rearrange("p (g c) -> p g c", g=SGG) for a in (stmp, sv))
                link(tt(s3, v3, over(w00[:, 0, :], P), ALU.mult))
                link(tt(s3, s3, over(w00[:, 1, :], P), ALU.add))
                signal(stt(stmp[r, :], stmp[r, :], 0.5, su[r, :], ALU.mult, ALU.mult), "gated")
                after(dve, PE, k, "gT")
                signal(cp(su[:, 0:SGG * NT], ps[0][:, 0:SGG * NT]), "gT")

            def unit(g):
                if g < N_SLOTS:
                    p = STEP_OF[g]
                    n, i = STEPS[p][0], g - SLOT0[p]
                    rows_h = h_rep if n % 3 == S else h_tok[n % 3]
                    if i == 0 and n % 3 == S:
                        after(dve, ACTE, WHERE[("norm", S, n // 3, 1)], "rep")
                        dve.wait_ge(route_in, 32 * NT * (n // 3 + 1))
                    dve.wait_ge(u_land[g % RING], 16 * (g // RING + 1))
                    u = uring[:, g % RING, :]
                    dve.tensor_tensor_reduce(u, u, rows_h[:, :], 1.0, 0.0, ALU.mult, ALU.add,
                                             dots[:, p % 2, i:i + 1]).then_inc(u_used, 1)
                if 0 < g <= N_SLOTS and g == SLOT0[STEP_OF[g - 1] + 1]:
                    p = STEP_OF[g - 1]
                    m = SLOTS[p]
                    dve.wait_ge(tanh_ready, p + 1)
                    if p >= 2:
                        dve.wait_ge(diag_ready, SLOT0[p - 1])
                    stt(wts[:, p % 2, 0:m], ew[:, 2, 0:m], 1.0, ew[:, 1, 0:m], ALU.add, ALU.mult).then_inc(w_ready, 1)
                if g < N_SLOTS and g == SLOT0[STEP_OF[g] + 1] - 1:
                    p = STEP_OF[g]
                    n, h = STEPS[p]
                    m = SLOTS[p]
                    dve.wait_ge(u_used, SLOT0[p + 1])
                    d = dots[:, p % 2, 0:m]
                    if p:
                        dve.wait_ge(w_ready, p)
                    polynomial(ew[:, 0, 0:m], d).then_inc(poly_ready, 1)
                    link(tt(ew[:, 1, 0:m], d, gate_s[:, :] if h is None else gate[n % 3][:, h, :], ALU.mult))

            def point(k, j):
                early_or_units(k, j, DVE, mod, lambda g: None, unit)

            stages = dict(init=init, tables=tables, mod=mod, norm=norm, mla_in=mla_in, attn=attn, proj=proj, query=query, topk_s=topk_s,
                          cache_init=cache_init, cache=cache, cache_out=cache_out, sgu_init=sgu_init,
                          sgu_vnorm=sgu_vnorm, sgu_mix=sgu_mix, sgu_s_mix=sgu_s_mix, sgu_out=sgu_out,
                          peer_out=peer_out)
            for k, s in enumerate(SCHEDULE):
                signals.start(k)
                if s[0] in stages:
                    stages[s[0]](k, *s[1:])
                else:
                    for j in range(n_points(k) - 1):
                        point(k, j)
                point(k, n_points(k) - 1)
                signals.end()


_INS = ["x_prompt", "x_sample", "c_prompt", "c_sample", "cache_kv_latent", "cache_k_rope", "page_table", "norm1_g",
        "norm2_g", "w_mod", "b_mod", "mla_w_in", "mla_g_q_a", "mla_g_kv_a", "mla_w_uq", "mla_g_q", "mla_w_uk",
        "mla_w_uv", "mla_g_k", "mla_w_o", "sg_w_in", "sg_b_in", "sg_g_v", "sg_w_s", "sg_b_s", "sg_w_out", "peer_w_q",
        "peer_sub_keys", "peer_u", "peer_v"]
_OUTS = {"y_prompt": (1, 256, D), "y_sample": (NT, 1, D), "new_kv_p": (1, 1, 256, KVR), "new_kr_p": (1, 1, 256, ROPE),
         "new_kv_s": (1, NT, 1, KVR), "new_kr_s": (1, NT, 1, ROPE), "new_v_p": (1, 1, P, SGH), "new_v_s": (1, NT, 1, SGH)}
_SCRATCH = {"modrows": ((2, 9, 6 * D), F32), "route_e": ((2, 64, TOPK), U32), "route_g": ((2, 64, TOPK), F32)}


def kernel(**inputs):
    import concourse.bacc as _bacc
    from concourse.bass_utils import run_bass_kernel_spmd as _run

    nc = _bacc.Bacc("TRN2", target_bir_lowering=False, num_devices=1)
    arrays, t = {}, {}

    def given(name, a):
        arrays[f"in_{name}"] = a
        t[name] = nc.dram_tensor(f"in_{name}", a.shape, mybir.dt.from_np(a.dtype), kind="ExternalInput").ap()

    for name in _INS:
        a = np.ascontiguousarray(inputs[name])
        if name == "cache_kv_latent":
            name, a = "cache_kv", a.reshape(-1, 8 * KVR)
        elif name == "cache_k_rope":
            name, a = "cache_kr", a.reshape(-1, 8 * ROPE)
        if name in ("peer_u", "peer_v"):
            for layer in range(2):
                given(f"{name}{layer}", a[layer])
            t[name] = [t[f"{name}{layer}"] for layer in range(2)]
        else:
            given(name, a)
    given("consts", constants())
    for name, shape in _OUTS.items():
        t[name] = nc.dram_tensor(f"out_{name}", shape, F32, kind="ExternalOutput").ap()
    for name, (shape, dt) in _SCRATCH.items():
        t[name] = nc.dram_tensor(name, shape, dt, kind="Internal").ap()
    program(nc, t)
    r = _run(nc, [arrays], core_ids=[0])
    return tuple(r.results[0][f"out_{name}"] for name in _OUTS)
```
